# Optimizing a Trainium2 kernel written in Bass

```python
import jax
import jax.numpy as jnp
from jax import lax
import numpy as np

D_MODEL = 1024
BATCH = 1
SEQ = 256
DEPTH = 2

GRID_W = 64
CTX_LEN = 256
HEAD_DIM = 64
Q_BLOCK = 128
ROPE_BASE = 10000.0
EPS = 1e-6
NEG_INF = -1e30
N_MOD = 9
FFN_RES = 0.5
D_FF = 2816

MLA_HEADS = 8
MLA_Q_RANK = 256
MLA_KV_RANK = 128
MLA_NOPE = 64
MLA_ROPE = 32
MLA_V = 64
GQA_HEADS = 8
GQA_KV_HEADS = 2
SWA_HEADS = 8
SWA_KV_HEADS = 2
WINDOW = 128
NA_HEADS = 8
NA_ROWS = 8
NA_COLS = 16

N_AB = (DEPTH + 1) // 2
N_CD = DEPTH // 2
AB_IN = MLA_Q_RANK + MLA_KV_RANK + MLA_ROPE + (GQA_HEADS + 2 * GQA_KV_HEADS) * HEAD_DIM
AB_OUT = MLA_HEADS * MLA_V + GQA_HEADS * HEAD_DIM
CD_IN = (SWA_HEADS + 2 * SWA_KV_HEADS) * HEAD_DIM + 3 * NA_HEADS * HEAD_DIM
CD_OUT = (SWA_HEADS + NA_HEADS) * HEAD_DIM

kernel_name = 'hybrid_mla_gqa_swa_na_macaron_dit'

def rms_norm(x, g):
    xf = x.astype(jnp.float32)
    y = xf * lax.rsqrt(jnp.mean(xf * xf, axis=-1, keepdims=True) + EPS)
    return y.astype(x.dtype) * g

def ada_in(x, mod, slot, g):
    return rms_norm(x, g) * (1 + mod[:, 3 * slot + 1, None, :]) + mod[:, 3 * slot, None, :]

def ada_out(x, y, mod, slot, g, w):
    return x + w * mod[:, 3 * slot + 2, None, :] * rms_norm(y, g)

def swiglu(h, wg, wu, wd):
    return (jax.nn.silu(h @ wg) * (h @ wu)) @ wd

def split_cols(t, sizes):
    return jnp.split(t, np.cumsum(sizes)[:-1].tolist(), axis=-1)

def axial_rope_tables(n_tok, rot_dim, dtype):
    t = jnp.arange(n_tok, dtype=jnp.int32)
    row = (t // GRID_W).astype(jnp.float32)
    col = (t % GRID_W).astype(jnp.float32)
    per_axis = rot_dim // 2
    inv = ROPE_BASE ** (-jnp.arange(0, per_axis, 2, dtype=jnp.float32) / per_axis)
    ang = jnp.concatenate([row[:, None] * inv, col[:, None] * inv], axis=-1)
    return jnp.cos(ang).astype(dtype), jnp.sin(ang).astype(dtype)

def apply_rope(x, cos, sin):
    x1, x2 = jnp.split(x, 2, axis=-1)
    cs, sn = cos[None, :, None, :], sin[None, :, None, :]
    return jnp.concatenate([x1 * cs - x2 * sn, x1 * sn + x2 * cs], axis=-1)

def neighbourhood_tables(rows):
    kr = min(NA_ROWS, rows)
    n_tok = rows * GRID_W
    t = jnp.arange(n_tok, dtype=jnp.int32)
    r, col = t // GRID_W, t % GRID_W
    r0 = jnp.clip(r - kr // 2, 0, rows - kr)
    c0 = jnp.clip(col - NA_COLS // 2, 0, GRID_W - NA_COLS)
    key_r = r0[:, None, None] + jnp.arange(kr, dtype=jnp.int32)[None, :, None]
    key_c = c0[:, None, None] + jnp.arange(NA_COLS, dtype=jnp.int32)[None, None, :]
    idx = (key_r * GRID_W + key_c).reshape(n_tok, kr * NA_COLS)
    rel = ((key_r - r[:, None, None] + NA_ROWS - 1) * (2 * NA_COLS - 1)
           + (key_c - col[:, None, None] + NA_COLS - 1)).reshape(n_tok, kr * NA_COLS)
    return idx, rel

def softmax_with_sink(logits, sink):
    if sink is None:
        return jax.nn.softmax(logits, axis=-1)
    s = jnp.broadcast_to(sink.astype(jnp.float32), logits.shape[:-1] + (1,))
    return jax.nn.softmax(jnp.concatenate([logits, s], axis=-1), axis=-1)[..., :-1]

def dense_gqa(q, k, v, sink=None):
    B, Q, H, d = q.shape
    Hk = k.shape[2]
    qg = q.reshape(B, Q, Hk, H // Hk, d)
    logits = jnp.einsum('bqhgd,bkhd->bhgqk', qg, k).astype(jnp.float32) * (d ** -0.5)
    p = softmax_with_sink(logits, sink).astype(v.dtype)
    o = jnp.einsum('bhgqk,bkhd->bqhgd', p, v)
    return o.reshape(B, Q, H, v.shape[-1])

def to_blocks(q):
    B, S, H, d = q.shape
    return q.reshape(B, S // Q_BLOCK, Q_BLOCK, H, d).transpose(1, 0, 2, 3, 4)

def from_blocks(o):
    nb, B, QB, H, d = o.shape
    return o.transpose(1, 0, 2, 3, 4).reshape(B, nb * QB, H, d)

def blocked_dense(q, k, v):
    return from_blocks(lax.map(lambda qi: dense_gqa(qi, k, v), to_blocks(q)))

def windowed_gqa(q, k, v, kc, vc, sink):
    B, S, H, d = q.shape
    Hk = k.shape[2]
    G = H // Hk
    nc = kc.shape[1]
    span = Q_BLOCK + 2 * WINDOW
    pad = ((0, 0), (WINDOW, WINDOW), (0, 0), (0, 0))
    kp, vp = jnp.pad(k, pad), jnp.pad(v, pad)
    scale = d ** -0.5

    def block(args):
        qi, b = args
        start = b * Q_BLOCK
        kw = lax.dynamic_slice_in_dim(kp, start, span, axis=1)
        vw = lax.dynamic_slice_in_dim(vp, start, span, axis=1)
        qpos = start + jnp.arange(Q_BLOCK, dtype=jnp.int32)
        kpos = start - WINDOW + jnp.arange(span, dtype=jnp.int32)
        valid = ((jnp.abs(qpos[:, None] - kpos[None, :]) <= WINDOW)
                 & (kpos[None, :] >= 0) & (kpos[None, :] < S))
        qg = qi.reshape(B, Q_BLOCK, Hk, G, d)
        lc = jnp.einsum('bqhgd,bkhd->bhgqk', qg, kc).astype(jnp.float32) * scale
        lw = jnp.einsum('bqhgd,bkhd->bhgqk', qg, kw).astype(jnp.float32) * scale
        lw = jnp.where(valid, lw, NEG_INF)
        p = softmax_with_sink(jnp.concatenate([lc, lw], axis=-1), sink).astype(v.dtype)
        o = (jnp.einsum('bhgqk,bkhd->bqhgd', p[..., :nc], vc)
             + jnp.einsum('bhgqk,bkhd->bqhgd', p[..., nc:], vw))
        return o.reshape(B, Q_BLOCK, H, v.shape[-1])

    nb = S // Q_BLOCK
    return from_blocks(lax.map(block, (to_blocks(q), jnp.arange(nb, dtype=jnp.int32))))

def neighbourhood_attend(q, k, v, kc, vc, rpb, nbr_idx, rel_idx):
    B, S, H, d = q.shape
    nb = S // Q_BLOCK
    nk = nbr_idx.shape[1]
    nc = kc.shape[1]
    rpb_flat = rpb.reshape(H, -1)
    scale = d ** -0.5

    def block(args):
        qi, idx, rel = args
        kn, vn = k[:, idx], v[:, idx]
        lc = jnp.einsum('bqhd,bkhd->bhqk', qi, kc).astype(jnp.float32) * scale
        ln = (jnp.einsum('bqhd,bqkhd->bhqk', qi, kn).astype(jnp.float32) * scale
              + rpb_flat[:, rel].astype(jnp.float32)[None])
        p = jax.nn.softmax(jnp.concatenate([lc, ln], axis=-1), axis=-1).astype(v.dtype)
        return (jnp.einsum('bhqk,bkhd->bqhd', p[..., :nc], vc)
                + jnp.einsum('bhqk,bqkhd->bqhd', p[..., nc:], vn))

    xs = (to_blocks(q), nbr_idx.reshape(nb, Q_BLOCK, nk), rel_idx.reshape(nb, Q_BLOCK, nk))
    return from_blocks(lax.map(block, xs))

def ab_mixer(h, hc, w_in, q_norm, w_uq, kv_norm, w_ukv, qn_b, kn_b, w_out, rope_a, rope_h, with_ctx):
    sizes = [MLA_Q_RANK, MLA_KV_RANK, MLA_ROPE, GQA_HEADS * HEAD_DIM,
             GQA_KV_HEADS * HEAD_DIM, GQA_KV_HEADS * HEAD_DIM]

    def project(t, positional):
        Bt, N, _ = t.shape
        cq, ckv, kr, bq, bk, bv = split_cols(t @ w_in, sizes)
        qa = (rms_norm(cq, q_norm) @ w_uq).reshape(Bt, N, MLA_HEADS, MLA_NOPE + MLA_ROPE)
        q_nope, q_rope = jnp.split(qa, [MLA_NOPE], axis=-1)
        kva = (rms_norm(ckv, kv_norm) @ w_ukv).reshape(Bt, N, MLA_HEADS, MLA_NOPE + MLA_V)
        k_nope, va = jnp.split(kva, [MLA_NOPE], axis=-1)
        kr = kr[:, :, None, :]
        bq = rms_norm(bq.reshape(Bt, N, GQA_HEADS, HEAD_DIM), qn_b)
        bk = rms_norm(bk.reshape(Bt, N, GQA_KV_HEADS, HEAD_DIM), kn_b)
        bv = bv.reshape(Bt, N, GQA_KV_HEADS, HEAD_DIM)
        if positional:
            q_rope = apply_rope(q_rope, *rope_a)
            kr = apply_rope(kr, *rope_a)
            bq = apply_rope(bq, *rope_h)
            bk = apply_rope(bk, *rope_h)
        qa = jnp.concatenate([q_nope, q_rope], axis=-1)
        ka = jnp.concatenate([k_nope, jnp.broadcast_to(kr, (Bt, N, MLA_HEADS, MLA_ROPE))], axis=-1)
        return qa, ka, va, bq, bk, bv

    B, S, _ = h.shape
    qa, ka, va, bq, bk, bv = project(h, True)
    qa_c, ka_c, va_c, bq_c, bk_c, bv_c = project(hc, False)
    o_a = blocked_dense(qa, jnp.concatenate([ka_c, ka], axis=1), jnp.concatenate([va_c, va], axis=1))
    o_b = blocked_dense(bq, jnp.concatenate([bk_c, bk], axis=1), jnp.concatenate([bv_c, bv], axis=1))
    y = jnp.concatenate([o_a.reshape(B, S, -1), o_b.reshape(B, S, -1)], axis=-1) @ w_out
    yc = None
    if with_ctx:
        Bc, N = hc.shape[:2]
        oc_a = dense_gqa(qa_c, ka_c, va_c)
        oc_b = dense_gqa(bq_c, bk_c, bv_c)
        yc = jnp.concatenate([oc_a.reshape(Bc, N, -1), oc_b.reshape(Bc, N, -1)], axis=-1) @ w_out
    return y, yc

def cd_mixer(h, hc, w_in, sink, rpb, w_out, rope_h, nbr_idx, rel_idx, with_ctx):
    sizes = [SWA_HEADS * HEAD_DIM, SWA_KV_HEADS * HEAD_DIM, SWA_KV_HEADS * HEAD_DIM,
             NA_HEADS * HEAD_DIM, NA_HEADS * HEAD_DIM, NA_HEADS * HEAD_DIM]

    def project(t, positional):
        Bt, N, _ = t.shape
        parts = split_cols(t @ w_in, sizes)
        cq, ck, cv, dq, dk, dv = [u.reshape(Bt, N, -1, HEAD_DIM) for u in parts]
        if positional:
            cq = apply_rope(cq, *rope_h)
            ck = apply_rope(ck, *rope_h)
        return cq, ck, cv, dq, dk, dv

    B, S, _ = h.shape
    sink_g = sink.reshape(1, SWA_KV_HEADS, SWA_HEADS // SWA_KV_HEADS, 1, 1)
    cq, ck, cv, dq, dk, dv = project(h, True)
    cq_c, ck_c, cv_c, dq_c, dk_c, dv_c = project(hc, False)
    o_c = windowed_gqa(cq, ck, cv, ck_c, cv_c, sink_g)
    o_d = neighbourhood_attend(dq, dk, dv, dk_c, dv_c, rpb, nbr_idx, rel_idx)
    y = jnp.concatenate([o_c.reshape(B, S, -1), o_d.reshape(B, S, -1)], axis=-1) @ w_out
    yc = None
    if with_ctx:
        Bc, N = hc.shape[:2]
        oc_c = dense_gqa(cq_c, ck_c, cv_c, sink_g)
        oc_d = dense_gqa(dq_c, dk_c, dv_c)
        yc = jnp.concatenate([oc_c.reshape(Bc, N, -1), oc_d.reshape(Bc, N, -1)], axis=-1) @ w_out
    return y, yc

def setup_inputs(seed: int = 0) -> dict:
    key = jax.random.key(seed)
    ks = jax.random.split(key, 24)
    f32 = jnp.float32

    def nrm(k, shape, fan_in, s=1.0):
        return jax.random.normal(k, shape, f32) * (s * fan_in ** -0.5)

    def gain(k, shape):
        return 1.0 + 0.1 * jax.random.normal(k, shape, f32)

    return {
        'x': jax.random.normal(ks[0], (BATCH, SEQ, D_MODEL), f32),
        'c': jax.random.normal(ks[1], (BATCH, D_MODEL), f32),
        'ctx': jax.random.normal(ks[2], (BATCH, CTX_LEN, D_MODEL), f32),
        'c_ctx': jax.random.normal(ks[3], (D_MODEL,), f32),
        'ada_w': nrm(ks[4], (DEPTH, D_MODEL, N_MOD * D_MODEL), D_MODEL, 0.5),
        'ada_b': 0.02 * jax.random.normal(ks[5], (DEPTH, N_MOD * D_MODEL), f32),
        'norm_g': gain(ks[6], (DEPTH, 6, D_MODEL)),
        'ffn_w_gate': nrm(ks[7], (DEPTH, 2, D_MODEL, D_FF), D_MODEL),
        'ffn_w_up': nrm(ks[8], (DEPTH, 2, D_MODEL, D_FF), D_MODEL),
        'ffn_w_down': nrm(ks[9], (DEPTH, 2, D_FF, D_MODEL), D_FF),
        'ab_w_in': nrm(ks[10], (N_AB, D_MODEL, AB_IN), D_MODEL),
        'mla_q_norm': gain(ks[11], (N_AB, MLA_Q_RANK)),
        'mla_w_uq': nrm(ks[12], (N_AB, MLA_Q_RANK, MLA_HEADS * (MLA_NOPE + MLA_ROPE)), MLA_Q_RANK),
        'mla_kv_norm': gain(ks[13], (N_AB, MLA_KV_RANK)),
        'mla_w_ukv': nrm(ks[14], (N_AB, MLA_KV_RANK, MLA_HEADS * (MLA_NOPE + MLA_V)), MLA_KV_RANK),
        'gqa_q_norm': gain(ks[15], (N_AB, HEAD_DIM)),
        'gqa_k_norm': gain(ks[16], (N_AB, HEAD_DIM)),
        'ab_w_out': nrm(ks[17], (N_AB, AB_OUT, D_MODEL), AB_OUT),
        'cd_w_in': nrm(ks[18], (N_CD, D_MODEL, CD_IN), D_MODEL),
        'swa_sink': jax.random.normal(ks[19], (N_CD, SWA_HEADS), f32),
        'na_rpb': 0.1 * jax.random.normal(ks[20], (N_CD, NA_HEADS, 2 * NA_ROWS - 1, 2 * NA_COLS - 1), f32),
        'cd_w_out': nrm(ks[21], (N_CD, CD_OUT, D_MODEL), CD_OUT),
    }

def reference(x, c, ctx, c_ctx, ada_w, ada_b, norm_g, ffn_w_gate, ffn_w_up, ffn_w_down,
              ab_w_in, mla_q_norm, mla_w_uq, mla_kv_norm, mla_w_ukv, gqa_q_norm, gqa_k_norm,
              ab_w_out, cd_w_in, swa_sink, na_rpb, cd_w_out):
    B, S, _ = x.shape
    rows = S // GRID_W
    rope_a = axial_rope_tables(S, MLA_ROPE, x.dtype)
    rope_h = axial_rope_tables(S, HEAD_DIM, x.dtype)
    nbr_idx, rel_idx = neighbourhood_tables(rows)
    s_lat = jax.nn.silu(c)
    s_ctx = jax.nn.silu(c_ctx)[None]
    xc = ctx
    for l in range(DEPTH):
        with_ctx = l < DEPTH - 1
        mod = (s_lat @ ada_w[l] + ada_b[l]).reshape(B, N_MOD, -1)
        mod_c = (s_ctx @ ada_w[l] + ada_b[l]).reshape(1, N_MOD, -1)
        g = norm_g[l]
        w1 = (ffn_w_gate[l, 0], ffn_w_up[l, 0], ffn_w_down[l, 0])
        w2 = (ffn_w_gate[l, 1], ffn_w_up[l, 1], ffn_w_down[l, 1])
        x = ada_out(x, swiglu(ada_in(x, mod, 0, g[0]), *w1), mod, 0, g[1], FFN_RES)
        xc = ada_out(xc, swiglu(ada_in(xc, mod_c, 0, g[0]), *w1), mod_c, 0, g[1], FFN_RES)
        h = ada_in(x, mod, 1, g[2])
        hc = ada_in(xc, mod_c, 1, g[2])
        i = l // 2
        if l % 2 == 0:
            y, yc = ab_mixer(h, hc, ab_w_in[i], mla_q_norm[i], mla_w_uq[i], mla_kv_norm[i],
                             mla_w_ukv[i], gqa_q_norm[i], gqa_k_norm[i], ab_w_out[i],
                             rope_a, rope_h, with_ctx)
        else:
            y, yc = cd_mixer(h, hc, cd_w_in[i], swa_sink[i], na_rpb[i], cd_w_out[i],
                             rope_h, nbr_idx, rel_idx, with_ctx)
        x = ada_out(x, y, mod, 1, g[3], 1.0)
        x = ada_out(x, swiglu(ada_in(x, mod, 2, g[4]), *w2), mod, 2, g[5], FFN_RES)
        if with_ctx:
            xc = ada_out(xc, yc, mod_c, 1, g[3], 1.0)
            xc = ada_out(xc, swiglu(ada_in(xc, mod_c, 2, g[4]), *w2), mod_c, 2, g[5], FFN_RES)
    return x


_drawn_inputs = setup_inputs


def setup_inputs(seed=0):
    import zlib

    import numpy as np

    out = dict(_drawn_inputs(seed))
    spreads = {}
    factors = {'mla_q_norm': 5.154,
     'gqa_q_norm': 7.663,
     'gqa_k_norm': 5.726,
     'swa_sink': 8.0,
     'na_rpb': 8.0}
    for name, (base, spread) in spreads.items():
        noise = np.random.default_rng([zlib.crc32(name.encode()), seed]).standard_normal(out[name].shape)
        drawn = base * np.exp(spread * noise) if base else spread * noise
        out[name] = jnp.asarray(drawn.astype(out[name].dtype))
    for name, factor in factors.items():
        out[name] = (out[name] * factor).astype(out[name].dtype)
    return out
```

```python
import concourse.bass as bass
from concourse import mybir
from contextlib import ExitStack
import numpy as np

F32 = mybir.dt.float32
F32R = mybir.dt.float32r
ALU = mybir.AluOpType
ACT = mybir.ActivationFunctionType
AX_X = mybir.AxisListType.X

P = 128
D = 1024
KD = D // P
LAT = 256
CTX = 256
NT = LAT + CTX
DFF = 2816
NF = DFF // P
LAYERS = 2
EPS = 1e-6
UW = 2048
UF = UW // KD
GU_STEPS = DFF // UF
DOWN_UNITS = NF * D // UW
ADA_W = 512
ADA_CH = ADA_W // P
ADA_K = 2
ADA_PCS = KD // ADA_K
ADA_PRO = 4
ADA_ALL = LAYERS * 9 * D // ADA_W
ADA_FFN = 7
ADA_MIX = (15, 5)
DEEP = 3
POOL_CH = 6
HD = 64
QK = 96
MLA_SCALE = float(QK) ** -0.5
HD_SCALE = float(HD) ** -0.5
GRID = 64
NEG = -1e30

C_ADAB, C_NORM, C_C, C_CC, C_QN, C_KVN, C_GQ, C_GK = 0, 144, 240, 248, 256, 258, 259, 260
N_COLS = 264

K_ID, K_ONE, K_KEEP = 0, 128, 256
M_BLK, M_P64, M_P96, M_C64, M_S64, M_C96, M_S96, M_END0 = 0, 128, 256, 384, 640, 896, 1152, 1408
M_SWA, M_NA, M_END1 = 1408, 1920, 1984


def constants():
    k = np.zeros((P, K_KEEP + M_END1), np.float32)
    k[:, K_ID:K_ID + P] = np.eye(P)
    k[:, K_ONE:K_ONE + P] = 1.0
    m = k[:, K_KEEP:]
    blk = np.arange(P) // HD
    m[:, M_BLK:M_BLK + P] = blk[:, None] == blk[None, :]
    for o in range(P):
        first = o % HD < HD // 2
        m[o + 32 if first else o - 32, M_P64 + o] = -1.0 if first else 1.0
    for o in range(64, QK):
        first = o < 80
        m[o + 16 if first else o - 16, M_P96 + o] = -1.0 if first else 1.0
    tok = np.arange(LAT)
    row, col = (tok // GRID).astype(np.float32), (tok % GRID).astype(np.float32)

    def angles(rot):
        per_axis = rot // 2
        inv = np.float32(10000.0) ** (-np.arange(0, per_axis, 2, dtype=np.float32) / np.float32(per_axis))
        return np.concatenate([row[:, None] * inv, col[:, None] * inv], -1).astype(np.float32)

    a64, a32 = angles(HD).T, angles(32).T
    m[:, M_C64:M_C64 + LAT] = np.cos(a64)[np.arange(P) % 32]
    m[:, M_S64:M_S64 + LAT] = np.sin(a64)[np.arange(P) % 32]
    m[64:QK, M_C96:M_C96 + LAT] = np.cos(a32)[np.arange(32) % 16]
    m[64:QK, M_S96:M_S96 + LAT] = np.sin(a32)[np.arange(32) % 16]
    for t in range(2):
        far = np.abs((t * P + np.arange(P))[:, None] - tok[None, :]) > 128
        m[:, M_SWA + t * LAT:M_SWA + (t + 1) * LAT] = np.where(far, NEG, 0.0)
    qc = np.arange(P) % GRID
    c0 = np.clip(qc - 8, 0, GRID - 16)
    kc = np.arange(GRID)
    m[:, M_NA:M_NA + GRID] = np.where((kc[None] >= c0[:, None]) & (kc[None] < c0[:, None] + 16), 0.0, NEG)
    return k


class Steps:

    def __init__(self, names, base):
        self.value = {n: base + i + 1 for i, n in enumerate(names)}
        self.next = base
        self.end = base + len(names)

    def at(self, *name):
        return self.value[name]

    def did(self, sem, instruction, *name):
        self.next += 1
        assert self.value[name] == self.next, name
        instruction.then_inc(sem, 1)



def mixer_tokens(layer, block):
    tok = []
    tiles = 4 if layer == 0 else 2
    items = [(p, e, t) for p in range(8) for e in range(2) for t in range(tiles)]

    def prep(p):
        if layer == 0 and p < 4:
            out = []
            for e in range(2):
                out += [("proj", "q", 2 * p + e), ("proj", "k", 2 * p + e), ("rope", "q", 2 * p + e)]
            if p == 3:
                out += [("split", 4), ("split", 5)]
            return out
        out = []
        if layer == 0:
            if p == 4:
                out += [("proj", "bk", 0), ("norm", "bk", 0), ("rope", "bk", 0), ("dup", "bk", 0),
                        ("proj", "bv", 0), ("split", 6)]
            out += [("proj", "bq", p), ("norm", "bq", p), ("rope", "bq", p)]
            if p == 5:
                out += [("split", 7)]
            if p == 7:
                out += [("split", 8)]
            return out
        if p < 4:
            out += [("proj", "cq", p), ("rope", "cq", p)]
        else:
            out += [("proj", "dq", p)]
        if p in (1, 3, 5, 7):
            out += [("split", 7 + (p - 1) // 2)]
        return out

    if layer == 0:
        tok += [("proj", "cq", 0), ("proj", "cq", 1), ("split", 2), ("proj", "ckv", 0), ("proj", "kr", 0),
                ("split", 3), ("rank", "cq", 0), ("rank", "ckv", 0), ("rope", "kr", 0), ("dup", "kr", 0)]
        tok += [("ada", block * ADA_PCS + j) for j in range(ADA_PCS)]
        tok += [("proj", "va", t) for t in range(4)]
        tok += [("flip", block)]
    else:
        tok += [("proj", "ck", 0), ("rope", "ck", 0), ("dup", "ck", 0), ("proj", "cv", 0), ("split", 2)]
        for u in range(2):
            tok += [("proj", "dv", 2 * u), ("proj", "dv", 2 * u + 1), ("split", 3 + u)]
        for u in range(2):
            tok += [("proj", "dk", 2 * u), ("proj", "dk", 2 * u + 1), ("split", 5 + u)]
    tok += prep(0)
    tok += [("score", 0), ("score", 1)]
    per_pair = 2 * tiles
    waiting, flip = prep(1), None
    pieces = ADA_MIX[layer] * ADA_PCS
    pieces0 = extra = ADA_PCS if layer == 0 else 0
    for i in range(len(items) + 1):
        if i < len(items):
            if i % per_pair == per_pair - 1:
                waiting = prep(i // per_pair + 2) if i // per_pair + 2 < 8 else []
            tok.append(("prob", i))
            if flip is not None:
                tok.append(("flip", flip))
                flip = None
            left = (per_pair - 2 - i) % per_pair + 1
            for _ in range(-(-len(waiting) // left)):
                tok.append(waiting.pop(0))
            while flip is None and extra < min(pieces, pieces0 + -(-(i + 1) * (pieces - pieces0) // (len(items) - 8))):
                tok.append(("ada", block * ADA_PCS + extra))
                extra += 1
                if extra % ADA_PCS == 0:
                    flip = block + extra // ADA_PCS - 1
            if i + 2 < len(items):
                tok.append(("score", i + 2))
            tok.append(("turn", i))
        if i >= 1:
            tok.append(("value", i - 1))
            p, e, t = items[i - 1]
            if e == 1 and t == tiles - 1:
                tok.append(("out", p))
    if flip is not None:
        tok.append(("flip", flip))
    assert extra == pieces
    return tok, items


def pe_steps(t, layer):
    k = t[0]
    if k == "rank":
        return [("sum",) + t[1:]]
    if k == "norm":
        return [("sum",) + t[1:]]
    if k in ("proj", "rope", "score", "turn", "value"):
        return [t]
    return []


def act_steps(t, layer):
    k = t[0]
    if k in ("rank", "norm"):
        n = 2 if t[1] == "cq" else 1
        out = [("square", t[1], t[2], c) for c in range(n)] + [("root",) + t[1:]]
        if k == "rank":
            out += [("hi", t[1], c) for c in range(n)]
        return out
    if k == "score":
        return [("exp", t[1])] + ([("sinkexp", t[1])] if layer == 1 and t[1] < 16 else [])
    if k == "turn":
        return [t]
    if k == "out":
        return [t]
    return []


def dve_steps(t, layer):
    k = t[0]
    if k == "proj":
        return [t]
    if k == "rank":
        n = 2 if t[1] == "cq" else 1
        return [("inv",) + t[1:]] + [("scaled", t[1], c) for c in range(n)] + [("lo", t[1], c) for c in range(n)]
    if k == "norm":
        return [("inv",) + t[1:], ("normed",) + t[1:]]
    if k == "rope":
        return [("sin",) + t[1:], ("cos",) + t[1:], t]
    if k == "dup":
        return [t]
    if k == "score":
        out = [("bias", t[1])] if layer == 1 else []
        out += [("max", t[1])]
        if layer == 1 and t[1] < 16:
            out += [("sinkmax", t[1])]
        return out
    if k == "prob":
        out = [("total", t[1])] if layer == 1 and t[1] < 16 else []
        return out + [("inv", t[1]), ("prob", t[1])]
    if k == "out":
        return [t]
    return []


def dit_kernel(nc, x, c, ctx_x, c_ctx, ada_w, ada_b, norm_g, ffn_w_gate, ffn_w_up, ffn_w_down,
               ab_w_in, mla_q_norm, mla_w_uq, mla_kv_norm, mla_w_ukv, gqa_q_norm, gqa_k_norm,
               ab_w_out, cd_w_in, swa_sink, na_rpb, cd_w_out, consts, out):
    es = ExitStack()
    with es:
        def sb(name, shape, dt=F32):
            return es.enter_context(nc.sbuf_tensor(name, shape, dt))

        def sem(name):
            return es.enter_context(nc.semaphore(name))

        X = sb("X", [P, KD, NT])
        raw = [sb(f"raw{s}", [P, UW]) for s in range(2)]
        wsp = [sb(f"wsp{s}", [P, 2, UW], F32R) for s in range(2)]
        with nc.sbuf_tensor("ada_raw", [P, 2, ADA_K, ADA_W], F32) as ada_raw:
            pass
        ada_lo = sb("ada_lo", [P, 2, ADA_K, ADA_W], F32R)
        with nc.sbuf_tensor("arow", [4, ADA_W], F32) as arow:
            pass
        ada_hi = sb("ada_hi", [P, ADA_K, ADA_W], F32R)
        T = [sb(f"T{i}", [P, NT]) for i in range(4)]
        R = T[3]
        cst = sb("cst", [P, K_KEEP])
        cols = sb("cols", [P, N_COLS])
        mod = sb("mod", [P, LAYERS * 72, 2])
        sT = sb("sT", [P, KD, 4])
        sS = sb("sS", [P, KD, 4], F32R)
        fold = sb("fold", [4, 2])
        gcol = sb("gcol", [P, KD, 2])
        scol = sb("scol", [P, KD, 2])
        epsc = sb("epsc", [P, 1])
        nmax = sb("nmax", [P, DEEP])
        psum_ = sb("psum_", [P, DEEP])
        pinv = sb("pinv", [P, DEEP])
        smax = sb("smax", [P, DEEP])
        sexp = sb("sexp", [P, DEEP])
        sinkc = sb("sinkc", [P, 8])
        ident, ones = cst[:, K_ID:K_ID + P], cst[:, K_ONE:K_ONE + P]

        with nc.sbuf_tensor("Ysb", [P, KD, NT], F32) as Ysb:
            pass
        with nc.sbuf_tensor("h_whole", [P, KD, 2, NT], F32) as h_whole:
            pass
        H = sb("H", [P, KD, 2, NT], F32R)
        with nc.sbuf_tensor("ada_pro", [P, KD, ADA_PRO * ADA_W], F32) as ada_pro:
            pass
        with nc.sbuf_tensor("rows", [P, 3, P], F32) as _:
            pass
        with ExitStack() as m0:
            def sm(name, shape, dt=F32):
                return m0.enter_context(nc.sbuf_tensor(name, shape, dt))
            sm("keep0", [P, KD, 2, NT])
            mc0 = sm("mc0", [P, M_END0])
            kdup0 = [sm(f"kdup0{g}", [P, NT]) for g in range(2)]
            va = sm("va", [P, 4, 512])
            vb = sm("vb", [P, 4, P])
            cqn = sm("cqn", [P, 2, 2, NT], F32R)
            ckvn = sm("ckvn", [P, 2, NT], F32R)
            qh0 = [sm(f"qh0{i}", [P, NT]) for i in range(4)]
            kh0 = [sm(f"kh0{i}", [P, NT]) for i in range(4)]
            p0 = sm("p0", [P, NT])
            Rm = sm("Rm", [P, NT])
            pt0 = [sm(f"pt0{i}", [P, 4, P]) for i in range(2)]
        with ExitStack() as m1:
            def sm(name, shape, dt=F32):
                return m1.enter_context(nc.sbuf_tensor(name, shape, dt))
            sm("keep1", [P, KD, 2, NT])
            mc1 = sm("mc1", [P, M_END1])
            toe = sm("toe", [P, 8, 6, GRID])
            kdup1 = [sm(f"kdup1{g}", [P, NT]) for g in range(2)]
            dk = sm("dk", [P, 4, NT])
            dv = sm("dv", [P, 4, 512])
            cv = sm("cv", [P, 4, P])
            qh1 = [sm(f"qh1{i}", [P, LAT]) for i in range(2)]
            p1 = [sm(f"p1{i}", [P, NT]) for i in range(2)]
            pt1 = [sm(f"pt1{i}", [P, 4, P]) for i in range(2)]
        A = sb("A", [P, NF, 2, NT], F32R)
        probs = ([p0, T[2], T[3]], p1 + [T[2]])
        kbuf = {"bk": kh0[0], "ck": T[3]}
        rows = T[0][:, 0:3 * P].rearrange("p (a b) -> p a b", a=3)
        outs = Ysb[:, 0:4, :].rearrange("p (t a) n -> p t (a n)", t=2)

        ps = [es.enter_context(nc.psum_tensor(f"ps{b}", [P, 512], F32)) for b in range(8)]
        rpb_win = nc.dram_tensor("rpb_win", (8, 7, GRID, 127), F32).ap()

        consts_in = sem("consts_in")
        rows_in = sem("rows_in")
        x_in = sem("x_in")
        pro_in = [sem(f"pro_in{i}") for i in range(4)]
        w_in = [sem(f"w_in{s}") for s in range(2)]
        hi_ready = sem("hi_ready")
        lo_ready = sem("lo_ready")
        ada_in = [sem(f"ada_in{s}") for s in range(2)]
        ada_hi_ready = sem("ada_hi_ready")
        ada_lo_ready = sem("ada_lo_ready")
        ada_mm = sem("ada_mm")
        arow_ready = sem("arow_ready")
        ada_flip = sem("ada_flip")
        mod_ready = sem("mod_ready")
        pro_mm = sem("pro_mm")
        pro_row = sem("pro_row")
        pro_flip = sem("pro_flip")
        s_split = sem("s_split")
        rows_t = sem("rows_t")
        cols_ready = sem("cols_ready")
        s_ready = sem("s_ready")
        xt_done = sem("xt_done")
        x_loaded = sem("x_loaded")
        gate_done = sem("gate_done")
        silu_done = sem("silu_done")
        up_done = sem("up_done")
        prod_done = sem("prod_done")
        ahi_done = sem("ahi_done")
        alo_done = sem("alo_done")
        down_done = sem("down_done")
        y_done = sem("y_done")
        y_out = sem("y_out")
        sq1_ready = sem("sq1_ready")
        sq1_used = sem("sq1_used")
        sq2_ready = sem("sq2_ready")
        sq2_used = sem("sq2_used")
        root_ready = sem("root_ready")
        inv_ready = sem("inv_ready")
        gain_ready = sem("gain_ready")
        upd_ready = sem("upd_ready")
        x_ready = sem("x_ready")
        xd_ready = sem("xd_ready")
        ht_ready = sem("ht_ready")
        hv_ready = sem("hv_ready")
        hh_ready = sem("hh_ready")
        hl_ready = sem("hl_ready")
        mix_in = sem("mix_in")
        win_in = sem("win_in")
        toe_in = sem("toe_in")
        sink_in = sem("sink_in")
        toe_ready = sem("toe_ready")
        pe_step = sem("pe_step")
        act_step = sem("act_step")
        dve_step = sem("dve_step")
        ot_done = sem("ot_done")
        o_ready = sem("o_ready")
        out_done = sem("out_done")
        zero_ready = sem("zero_ready")

        MIX_IN = (7, 9)
        base, phase = 0, []
        for l in range(LAYERS):
            for kind in ("ffn0", "mix", "ffn1"):
                phase.append(base)
                base += 2 * GU_STEPS + DOWN_UNITS if kind != "mix" else MIX_IN[l] + 4
        phase.append(base)
        last_unit = base

        def kview(ap, lo_, n):
            return ap.rearrange("(k p) n -> p k n", p=P)[:, :, lo_:lo_ + n]

        w_ab, w_cd = ab_w_in[0], cd_w_in[0]
        mix_src = [
            [kview(w_ab, 0, 256), kview(w_ab, 256, 160), kview(mla_w_uq[0], 0, 768), kview(mla_w_ukv[0], 0, 1024),
             kview(w_ab, 928, 256), kview(w_ab, 416, 256), kview(w_ab, 672, 256)],
            [kview(w_cd, 512, 256), kview(w_cd, 1792, 256), kview(w_cd, 2048, 256), kview(w_cd, 1280, 256),
             kview(w_cd, 1536, 256), kview(w_cd, 0, 256), kview(w_cd, 256, 256), kview(w_cd, 768, 256),
             kview(w_cd, 1024, 256)],
        ]
        mix_out = [ab_w_out[0], cd_w_out[0]]

        def unit_width(n):
            for l in range(LAYERS):
                j = n - phase[3 * l + 1]
                if 0 <= j < MIX_IN[l]:
                    s = mix_src[l][j].shape
                    return s[1] * s[2]
            return UW

        ada_first, ada_norm = [], [None] * 6
        block = ADA_FFN
        for r in range(1, 6):
            ada_norm[r] = block
            block += 1
            if r % 3 == 1:
                ada_first.append(block)
                block += ADA_MIX[r // 3]
        assert ADA_PRO + block == ADA_ALL

        plans = []
        pe0 = act0 = dve0 = 0
        for l in range(LAYERS):
            toks, items = mixer_tokens(l, ada_first[l])
            pe = Steps([s for t in toks for s in pe_steps(t, l)], pe0)
            ac = Steps([s for t in toks for s in act_steps(t, l)], act0)
            dv_ = Steps([s for t in toks for s in dve_steps(t, l)], dve0)
            plans.append((toks, items, pe, ac, dv_))
            pe0, act0, dve0 = pe.end, ac.end, dv_.end

        unit_end = [
            {0: ("proj", "cq", 1), 1: ("proj", "kr", 0), 2: ("proj", "q", 7), 3: ("proj", "k", 7),
             4: ("proj", "bv", 0), 5: ("proj", "bq", 5), 6: ("proj", "bq", 7)},
            {0: ("proj", "cv", 0), 1: ("proj", "dv", 1), 2: ("proj", "dv", 3), 3: ("proj", "dk", 1),
             4: ("proj", "dk", 3), 5: ("proj", "cq", 1), 6: ("proj", "cq", 3), 7: ("proj", "dq", 5),
             8: ("proj", "dq", 7)},
        ]

        def work_order(l):
            o = []
            for t in plans[l][0]:
                if t[0] == "proj":
                    o.append((t, "dve", t))
                elif t[0] in ("rank", "norm"):
                    o.append((("sum",) + t[1:], "act", ("root",) + t[1:]))
                elif t[0] == "rope":
                    o.append((t, "dve", ("sin",) + t[1:]))
            return o
        work = [work_order(l) for l in range(LAYERS)]

        B_WORK, B_ADA, B_S, B_PT, B_O = (0, 1), 2, (3, 4, 5), 6, 7
        B_ADA_NORM = 6

        def work_bank(l, name):
            i = [u[0] for u in work[l]].index(name)
            return ps[B_WORK[i % len(B_WORK)]]
        NW_POST = (NT, NT, NT, NT, LAT, LAT)
        NW_PRE = (NT, NT, NT, NT, NT, LAT)

        def bank_of(ch):
            return (ch + 4) % 8

        PRO_BANKS = (4, 6, 7, 3)
        SS1, SS2 = 4, 5

        ada_cols = ada_w.rearrange("l (k p) n -> l p k n", p=P)

        def ada_landed(k):
            return ada_in[k % 2], 16 * (k // 2 + 1)

        ADA_SPLIT = ADA_FFN * ADA_PCS + 1

        def ada_load(eng, k):
            if k >= 2:
                eng.wait_ge(ada_mm, k - 1)
            l, c0 = divmod((ADA_PRO + k // ADA_PCS) * ADA_W, 9 * D)
            kk = ADA_K * (k % ADA_PCS)
            eng.dma_start(ada_raw[:, k % 2, :, :], ada_cols[l][:, kk:kk + ADA_K, c0:c0 + ADA_W]).then_inc(ada_landed(k)[0], 16)

        def x_landed(b, ch):
            if ch < POOL_CH:
                return x_ready, POOL_CH * b + ch + 1
            return xd_ready, (KD - POOL_CH) * b + ch - POOL_CH + 1

        def ada_blocks(m):
            return m // ADA_CH - ADA_PRO + 1

        def wviews(n, k):
            w = wsp[n % 2]
            width = unit_width(n)
            return [w[:, h, 0:width].rearrange("p (k n) -> p k n", k=k) for h in range(2)]

        block = es.enter_context(nc.Block())

        @block.sync
        def _(sp):
            sp.dma_start(cst[:], consts[:, 0:K_KEEP]).then_inc(consts_in, 16)
            ab2 = ada_b.rearrange("l (r n) -> (l r) n", n=P)
            sp.dma_start(rows[:, 0, :], ab2[0:P, :]).then_inc(rows_in, 16)
            sp.dma_start(rows[0:16, 1, :], ab2[P:P + 16, :]).then_inc(rows_in, 16)
            sp.dma_start(rows[16:112, 1, :], norm_g.rearrange("l g (r n) -> (l g r) n", n=P)).then_inc(rows_in, 16)
            sp.dma_start(rows[112:120, 1, :], c.rearrange("b (r n) -> (b r) n", n=P)).then_inc(rows_in, 16)
            sp.dma_start(rows[120:128, 1, :], c_ctx.rearrange("(r n) -> r n", n=P)).then_inc(rows_in, 16)
            sp.dma_start(rows[0:2, 2, :], mla_q_norm.rearrange("b (r n) -> (b r) n", n=P)).then_inc(rows_in, 16)
            sp.dma_start(rows[2:3, 2, :], mla_kv_norm).then_inc(rows_in, 16)
            for r, g in ((3, gqa_q_norm), (4, gqa_k_norm)):
                for h in range(2):
                    sp.dma_start(rows[r:r + 1, 2, h * HD:(h + 1) * HD], g).then_inc(rows_in, 16)
            sp.dma_start(sinkc[:], swa_sink.broadcast_to([P, 8])).then_inc(sink_in, 16)
            xr = x[0].rearrange("(t p) n -> p t n", p=P)
            cr = ctx_x[0].rearrange("(t p) n -> p t n", p=P)
            yrow = Ysb[:, :, :].rearrange("p (t a) n -> p t (a n)", t=4)
            sp.dma_start(yrow[:, 0:2, :], xr).then_inc(x_in, 16)
            sp.dma_start(yrow[:, 2:4, :], cr).then_inc(x_in, 16)
            for i in range(4):
                w = ADA_PRO * ADA_W // 4
                sp.dma_start(ada_pro[:, :, i * w:(i + 1) * w], kview(ada_w[0], i * w, w)).then_inc(pro_in[i], 16)

            def free(n):
                sp.wait_ge(hi_ready, n - 1)
                sp.wait_ge(lo_ready, n - 1)

            def load(n, src, k):
                dst = raw[n % 2][:, 0:src.shape[1] * src.shape[2]].rearrange("p (k n) -> p k n", k=k)
                sp.dma_start(dst, src).then_inc(w_in[n % 2], 16)

            def ada_beside(r):
                for j in range(ADA_PCS):
                    if ada_norm[r] * ADA_PCS + j + 2 < (ADA_ALL - ADA_PRO) * ADA_PCS:
                        ada_load(sp, ada_norm[r] * ADA_PCS + j + 2)

            def ffn(n0, l, s):
                gate = ffn_w_gate[l, s].rearrange("(k p) n -> p k n", p=P)
                up = ffn_w_up[l, s].rearrange("(k p) n -> p k n", p=P)
                down = ffn_w_down[l, s].rearrange("(f p) n -> p f n", p=P)
                if n0 == 0:
                    ada_load(sp, 0)
                    load(0, gate[:, :, 0:UF], KD)
                    load(1, up[:, :, 0:UF], KD)
                    ada_load(sp, 1)
                    free(2)
                    load(2, gate[:, :, UF:2 * UF], KD)
                    free(3)
                    load(3, up[:, :, UF:2 * UF], KD)
                    with sp.Fori(0, ADA_FFN) as i:
                        for j in range(ADA_PCS):
                            sp.wait_ge(ada_mm, ADA_PCS * i + j + 1)
                            kk = ADA_K * ((2 + j) % ADA_PCS)
                            src = ada_cols[0][:, kk:kk + ADA_K, bass.ds((ADA_PRO + (2 + j) // ADA_PCS) * ADA_W + i * ADA_W, ADA_W)]
                            sp.dma_start(ada_raw[:, j % 2, :, :], src).then_inc(ada_in[j % 2], 16)
                            if j % 2 == 1:
                                part = j // 2
                                sp.wait_ge(hi_ready, 2 * i + part + 3)
                                sp.wait_ge(lo_ready, 2 * i + part + 3)
                                load(part, (gate, up)[part][:, :, bass.ds(i * UF + 2 * UF, UF)], KD)
                else:
                    for j, w in enumerate((gate, up)):
                        free(n0 + j)
                        load(n0 + j, w[:, :, 0:UF], KD)
                    ada_beside(3 * l + 2 * s)
                with sp.Fori(ADA_FFN + 2 if n0 == 0 else 1, GU_STEPS) as i:
                    for j, w in enumerate((gate, up)):
                        sp.wait_ge(hi_ready, n0 + 2 * i + j - 1)
                        sp.wait_ge(lo_ready, n0 + 2 * i + j - 1)
                        load(n0 + j, w[:, :, bass.ds(i * UF, UF)], KD)
                n1 = n0 + 2 * GU_STEPS
                with sp.Fori(0, DOWN_UNITS // 2) as i:
                    for j in range(2):
                        sp.wait_ge(hi_ready, n1 + 2 * i + j - 1)
                        sp.wait_ge(lo_ready, n1 + 2 * i + j - 1)
                        load(n1 + j, down[:, bass.ds(4 * i + 2 * j, 2), :], 2)
                free(n1 + DOWN_UNITS - 1)
                load(n1 + DOWN_UNITS - 1, down[:, 2 * (DOWN_UNITS - 1):, :], 2)

            for l in range(LAYERS):
                ffn(phase[3 * l], l, 0)
                mc = (mc0, mc1)[l]
                n0 = phase[3 * l + 1]

                def mixer_unit(j):
                    free(n0 + j)
                    if j < MIX_IN[l]:
                        load(n0 + j, mix_src[l][j], mix_src[l][j].shape[1])
                    else:
                        f = 2 * (j - MIX_IN[l])
                        load(n0 + j, mix_out[l].rearrange("(f p) n -> p f n", p=P)[:, f:f + 2, :], 2)

                mixer_unit(0)
                mixer_unit(1)
                ada_beside(3 * l + 1)
                sp.wait_ge(y_done, 8 * (3 * l + 1))
                sp.dma_start(mc[:], consts[:, K_KEEP:K_KEEP + mc.shape[1]]).then_inc(mix_in, 16)
                mixer_unit(2)
                mixer_unit(3)
                for t in plans[l][0]:
                    if t[0] == "split":
                        mixer_unit(t[1] + 2)
                    elif t[0] == "ada" and t[1] + 2 < (ADA_ALL - ADA_PRO) * ADA_PCS:
                        ada_load(sp, t[1] + 2)
                ffn(phase[3 * l + 2], l, 1)
            for t in range(2):
                sp.wait_ge(o_ready, 2 * (t + 1))
                sp.dma_start(out[0, t * P:(t + 1) * P, :], outs[:, t, :]).then_inc(out_done, 16)
            sp.wait_ge(out_done, 32)

        @block.gpsimd
        def _(pool):
            def residual(b):
                w = NW_POST[b]
                for ch in range(POOL_CH):
                    pool.wait_ge(upd_ready, KD * b + ch + 1)
                    pool.tensor_tensor(X[:, ch, 0:w], X[:, ch, 0:w], Ysb[:, ch, 0:w], ALU.add).then_inc(x_ready, 1)

            def low(r):
                w = NW_PRE[r]
                for ch in range(KD):
                    pool.wait_ge(hh_ready, KD * r + ch + 1)
                    pool.tensor_tensor(H[:, ch, 1, 0:w], h_whole[:, ch, 1, 0:w], H[:, ch, 0, 0:w].bitcast(F32), ALU.subtract).then_inc(hl_ready, 1)

            for h in range(8):
                src = bass.AP(tensor=na_rpb.tensor, offset=na_rpb.offset + h * 465 + 4 * 31 + 15 - 63,
                              ap=[[31, 7], [0, GRID], [1, 127]])
                pool.dma_start(rpb_win[h], src).then_inc(win_in, 16)
            low(0)
            residual(0)
            low(1)
            residual(1)
            low(2)
            residual(2)
            low(3)
            pool.wait_ge(win_in, 16 * 8)
            pool.wait_ge(y_done, 8 * 4)
            for half in range(2):
                for h in range(8):
                    src = bass.AP(tensor=rpb_win.tensor,
                                  offset=rpb_win.offset + h * 7 * GRID * 127 + (1 - half) * GRID * 127 + 63 - GRID * 127 * 0,
                                  ap=[[126, GRID], [GRID * 127, 6], [1, GRID]])
                    pool.dma_start(toe[half * GRID:(half + 1) * GRID, h, :, :], src).then_inc(toe_in, 16)
            residual(3)
            low(4)
            pool.wait_ge(toe_in, 16 * 16)
            pool.wait_ge(mix_in, 32)
            mask = mc1[:, M_NA:M_NA + GRID].rearrange("p (a n) -> p a n", a=1).broadcast_to([P, 6, GRID])
            for h in range(8):
                pool.tensor_tensor(toe[:, h, :, :], toe[:, h, :, :], mask, ALU.add).then_inc(toe_ready, 1)
            residual(4)
            low(5)
            residual(5)

        @block.tensor
        def _(pe):
            mm = nc.tensor.matmul

            def mm3(o, w, v, start, stop):
                mm(o, w[0], v[0], start=start, stop=False)
                mm(o, w[0], v[1], start=False, stop=False)
                return mm(o, w[1], v[0], start=False, stop=stop)

            def hl(t, k, c0, c1):
                return t[:, k, 0, c0:c1], t[:, k, 1, c0:c1]

            def ada_piece(slot, j, bank, split):
                for kk in range(ADA_K):
                    k = ADA_K * j + kk
                    start, stop = k == 0, k == KD - 1
                    o = ps[bank][0:4, :]
                    if split:
                        mm(o, sS[:, k, :], ada_hi[:, kk, :], start=start, stop=False)
                        last = mm(o, sS[:, k, :], ada_lo[:, slot, kk, :], start=False, stop=stop)
                    else:
                        last = mm(o, sT[:, k, :], ada_raw[:, slot, kk, :], start=start, stop=stop)
                last.then_inc(ada_mm, 1)

            def ada_fold(bank, ch, row):
                return mm(ps[bank][:, 2 * ch:2 * ch + 2], row, fold[:], start=True, stop=True)

            def ada_turn(bank):
                for ch in range(ADA_CH):
                    last = ada_fold(bank, ch, arow[:, ch * P:(ch + 1) * P])
                last.then_inc(ada_flip, 1)

            def sum_sq(ready, used, bank, b, ch, w):
                pe.wait_ge(ready, KD * b + ch + 1)
                mm(ps[bank][:, 0:w], ones, T[ch % 2][:, 0:w], start=ch == 0, stop=ch == KD - 1).then_inc(used, 1)

            def pre_sums(r, w):
                for ch in range(KD):
                    if r and ch in (0, 2, 5):
                        for j in {0: (0, 1), 2: (2,), 5: (3,)}[ch]:
                            k = ada_norm[r] * ADA_PCS + j
                            if k < ADA_SPLIT:
                                pe.wait_ge(ada_lo_ready, k + 1)
                            else:
                                pe.wait_ge(*ada_landed(k))
                            if j == 0:
                                pe.wait_ge(y_out, KD * r)
                            ada_piece(k % 2, j, B_ADA_NORM, k < ADA_SPLIT)
                    sum_sq(sq2_ready, sq2_used, SS2, r, ch, w)
                if r:
                    pe.wait_ge(arow_ready, ada_norm[r] + 1)
                    ada_turn(B_ADA_NORM)

            def ffn(q, n0, r, l, s):
                w = NW_PRE[r]

                def gate_up(lo_, hi_, with_ada):
                    with pe.Fori(lo_, hi_) as i:
                        for part, (done, free) in enumerate(((gate_done, silu_done), (up_done, prod_done))):
                            pe.wait_ge(hi_ready, n0 + 2 * i + part + 1)
                            pe.wait_ge(lo_ready, n0 + 2 * i + part + 1)
                            W = wviews(n0 + part, KD)
                            for j in range(2):
                                pe.wait_ge(free, q * NF + 2 * i + j + 1)
                                o = ps[2 * part + j][:, 0:w]
                                for k in range(KD):
                                    if part == 0 and j == 0:
                                        pe.wait_ge(hl_ready, KD * r + k + 1)
                                    lw = [W[h][:, k, j * P:(j + 1) * P] for h in range(2)]
                                    pc = 2 * part + j
                                    if with_ada and k == 4:
                                        pe.wait_ge(ada_lo_ready, ADA_PCS * i + pc + 1)
                                        if pc == 0:
                                            pe.wait_ge(mod_ready, i + 1)
                                        ada_piece(j, pc, 4, True)
                                    if with_ada and k == KD - 1 and pc == 3:
                                        pe.wait_ge(arow_ready, i + 1)
                                    last = mm3(o, lw, hl(H, k, 0, w), k == 0, k == KD - 1)
                                last.then_inc(done, 1)
                            if with_ada and part == 1:
                                ada_turn(4)

                if q == 0:
                    gate_up(0, ADA_FFN, True)
                gate_up(ADA_FFN if q == 0 else 0, GU_STEPS, False)
                down(n0 + 2 * GU_STEPS, DOWN_UNITS, r, w, q)

            def down(n1, units, b, w, q):
                def unit(n, f0, start, stop, pair=None):
                    pe.wait_ge(hi_ready, n + 1)
                    pe.wait_ge(lo_ready, n + 1)
                    W = wviews(n if pair is None else pair, 2)
                    for ch in range(KD):
                        for f in range(2):
                            lw = [W[h][:, f, ch * P:(ch + 1) * P] for h in range(2)]
                            if isinstance(f0, int):
                                v = hl(A, f0 + f, 0, w)
                            else:
                                v = [A[:, bass.ds(f0 + f, 1), h, 0:w].rearrange("p a n -> p (a n)") for h in range(2)]
                            last = mm3(ps[bank_of(ch)][:, 0:w], lw, v, start and f == 0, stop and f == 1)
                        if stop:
                            last.then_inc(y_done, 1)
                            if ch >= 2:
                                sum_sq(sq1_ready, sq1_used, SS1, b, ch - 2, w)
                    if not stop:
                        last.then_inc(down_done, 1)

                if q is not None:
                    pe.wait_ge(mod_ready, ada_norm[b] + 2 if b else ADA_FFN + 1)
                    pe.wait_ge(silu_done, (q + 1) * NF + 2)
                    pe.wait_ge(alo_done, (q + 1) * NF + 2)
                unit(n1, 0, True, False)
                if units == DOWN_UNITS:
                    unit(n1 + 1, 2, False, False)
                    with pe.Fori(1, 4) as i:
                        for j in range(2):
                            unit(n1 + 2 * i + j, 4 * i + 2 * j, False, False, pair=n1 + j)
                    for u in (8, 9):
                        unit(n1 + u, 2 * u, False, False)
                else:
                    for u in range(1, units - 1):
                        unit(n1 + u, 2 * u, False, False)
                unit(n1 + units - 1, 2 * (units - 1), False, True)
                for ch in (6, 7):
                    sum_sq(sq1_ready, sq1_used, SS1, b, ch, w)

            def mixer(l, b):
                toks, items, st, ac, dv_ = plans[l]
                n0 = phase[b]
                mc = (mc0, mc1)[l]
                qh, kh, pp, pt = (qh0, kh0, probs[0], pt0) if l == 0 else (qh1, None, probs[1], pt1)
                kd_ = (kdup0, kdup1)[l]
                tiles = 4 if l == 0 else 2
                pe.wait_ge(mix_in, 16 * (l + 1))

                def use(j):
                    pe.wait_ge(hi_ready, n0 + j + 1)
                    pe.wait_ge(lo_ready, n0 + j + 1)
                    return wviews(n0 + j, mix_src[l][j].shape[1])

                def features(o, W, c0, m, w, h_waits=False):
                    for k in range(KD):
                        if h_waits:
                            pe.wait_ge(hl_ready, KD * b + k + 1)
                        last = mm3(o, [W[h][:, k, c0:c0 + m] for h in range(2)], hl(H, k, 0, w), k == 0, k == KD - 1)
                    return last

                def by_token(o, W, c0, n, t):
                    for k in range(KD):
                        last = mm3(o, [x_ for x_ in hl(H, k, t * P, (t + 1) * P)], [W[h][:, k, c0:c0 + n] for h in range(2)],
                                   k == 0, k == KD - 1)
                    return last

                def work_free(name):
                    i = [u[0] for u in work[l]].index(name) - len(B_WORK)
                    if i >= 0:
                        _, eng, reader = work[l][i]
                        pe.wait_ge(act_step if eng == "act" else dve_step, (ac if eng == "act" else dv_).at(*reader))

                first_proj = work[l][0][0]
                for t in toks:
                    k = t[0]
                    if k == "proj":
                        work_free(t)
                        h_waits = t is first_proj
                        o = work_bank(l, t)
                        what, j = t[1:]
                        if (l, what) == (0, "cq"):
                            last = features(o[:, 0:NT], use(0), j * P, P, NT, h_waits)
                        elif what == "ckv":
                            last = features(o[:, 0:NT], use(1), 0, P, NT)
                        elif what == "kr":
                            last = features(o[0:32, 0:NT], use(1), P, 32, NT)
                        elif what == "va":
                            W = use(3)
                            pe.wait_ge(dve_step, dv_.at("lo", "ckv", 0))
                            wv = [W[h][:, 0, :].rearrange("p (h e) -> p h e", e=P)[:, :, HD:P] for h in range(2)]
                            last = mm3(o[:, 0:512].rearrange("p (h e) -> p h e", e=HD),
                                       [ckvn[:, h, j * P:(j + 1) * P] for h in range(2)], wv, True, True)
                        elif what == "q":
                            W = use(2)
                            pe.wait_ge(dve_step, dv_.at("lo", "cq", 1))
                            for kk in range(2):
                                last = mm3(o[0:QK, 0:NT], [W[h][:, kk, j * QK:(j + 1) * QK] for h in range(2)],
                                           [cqn[:, kk, h, :] for h in range(2)], kk == 0, kk == 1)
                        elif what == "k":
                            W = use(3)
                            pe.wait_ge(dve_step, dv_.at("lo", "ckv", 0))
                            last = mm3(o[0:HD, 0:NT], [W[h][:, 0, j * P:j * P + HD] for h in range(2)],
                                       [ckvn[:, h, :] for h in range(2)], True, True)
                        elif what in ("bk", "ck"):
                            last = features(o[:, 0:NT], use(4 if l == 0 else 0), 0, P, NT, h_waits)
                        elif what in ("bv", "cv"):
                            W = use(4 if l == 0 else 0)
                            for tt in range(4):
                                last = by_token(o[:, tt * P:(tt + 1) * P], W, P, P, tt)
                        elif what == "bq":
                            last = features(o[:, 0:NT], use(5 + (j - 4) // 2), (j % 2) * P, P, NT)
                        elif what == "dv":
                            W = use(1 + j // 2)
                            for tt in range(2):
                                last = by_token(o[:, tt * 256:(tt + 1) * 256], W, 0, 256, 2 * (j % 2) + tt)
                        elif what == "dk":
                            last = features(o[:, 0:NT], use(3 + j // 2), (j % 2) * P, P, NT)
                        elif what == "cq":
                            last = features(o[:, 0:LAT], use(5 + j // 2), (j % 2) * P, P, LAT)
                        elif what == "dq":
                            last = features(o[:, 0:LAT], use(7 + (j - 4) // 2), (j % 2) * P, P, LAT)
                        st.did(pe_step, last, *t)
                    elif k in ("rank", "norm"):
                        name = ("sum",) + t[1:]
                        work_free(name)
                        n = 2 if t[1] == "cq" else 1
                        for i in range(n):
                            pe.wait_ge(act_step, ac.at("square", t[1], t[2], i))
                            lw = ones if k == "rank" else mc[:, M_BLK:M_BLK + P]
                            last = mm(work_bank(l, name)[:, 0:NT], lw, T[i][:, 0:NT], start=i == 0, stop=i == n - 1)
                        st.did(pe_step, last, *name)
                    elif k == "ada":
                        pe.wait_ge(*ada_landed(t[1]))
                        if t[1] % ADA_PCS == 0:
                            pe.wait_ge(mod_ready, t[1] // ADA_PCS + 1)
                            if t[1] // ADA_PCS == ada_first[l]:
                                pe.wait_ge(y_out, KD * b)
                        ada_piece(t[1] % 2, t[1] % ADA_PCS, B_ADA, False)
                    elif k == "flip":
                        pe.wait_ge(arow_ready, t[1] + 1)
                        ada_turn(B_ADA)
                    elif k == "rope":
                        work_free(t)
                        what, j = t[1:]
                        ax = work_bank(l, t)
                        if what == "q":
                            pe.wait_ge(dve_step, dv_.at("proj", "q", j))
                            last = mm(ax[0:QK, 0:LAT], mc[0:QK, M_P96:M_P96 + QK], qh[j % 4][0:QK, 0:LAT], start=True, stop=True)
                        elif what == "kr":
                            pe.wait_ge(dve_step, dv_.at("proj", "kr", 0))
                            last = mm(ax[0:QK, 0:LAT], mc[0:QK, M_P96:M_P96 + QK], T[3][0:QK, 0:LAT], start=True, stop=True)
                        else:
                            src = kbuf.get(what, qh[j % 2])
                            pe.wait_ge(dve_step, dv_.at("normed", what, j) if what[0] == "b" else dv_.at("proj", what, j))
                            last = mm(ax[:, 0:LAT], mc[:, M_P64:M_P64 + P], src[:, 0:LAT], start=True, stop=True)
                        st.did(pe_step, last, *t)
                    elif k == "score":
                        i = t[1]
                        p, e, tt = items[i]
                        if i >= DEEP:
                            pe.wait_ge(act_step, ac.at("exp", i - DEEP))
                        if l == 0 and p < 4:
                            h = 2 * p + e
                            pe.wait_ge(dve_step, max(dv_.at("rope", "q", h), dv_.at("proj", "k", h), dv_.at("dup", "kr", 0)))
                            lhs, rhs = qh[h % 4][0:QK, :], kh[h % 4][0:QK, :]
                        else:
                            g = slice(e * HD, (e + 1) * HD)
                            if l == 0 or p < 4:
                                need = ("rope", "bq" if l == 0 else "cq", p)
                                rhs = kd_[(p % 4) // 2][g, :]
                            else:
                                need = ("proj", "dq", p)
                                rhs = dk[g, p - 4, :]
                            pe.wait_ge(dve_step, dv_.at(*need))
                            lhs = qh[p % 2][g, :]
                        k0_ = 0 if tt < 2 else LAT
                        last = mm(ps[B_S[i % DEEP]][:, k0_:NT], lhs[:, tt * P:(tt + 1) * P], rhs[:, k0_:NT], start=True, stop=True)
                        st.did(pe_step, last, *t)
                    elif k == "turn":
                        i = t[1]
                        tt = items[i][2]
                        pe.wait_ge(dve_step, dv_.at("prob", i))
                        if i >= 1:
                            pe.wait_ge(act_step, ac.at("turn", i - 1))
                        for kt in range(0 if tt < 2 else 2, 4):
                            last = nc.tensor.transpose(ps[B_PT][:, kt * P:(kt + 1) * P], pp[i % DEEP][:, kt * P:(kt + 1) * P], ident)
                        st.did(pe_step, last, *t)
                    elif k == "value":
                        i = t[1]
                        p, e, tt = items[i]
                        pe.wait_ge(act_step, ac.at("turn", i))
                        if e == 0 and tt == 0 and p:
                            pe.wait_ge(dve_step, dv_.at("out", p - 1))
                        if l == 0:
                            v, c0 = (va, (2 * p + e) * HD) if p < 4 else (vb, ((p - 4) // 2) * HD)
                        else:
                            v, c0 = (cv, (p // 2) * HD) if p < 4 else (dv, (2 * (p - 4) + e) * HD)
                        first = 0 if tt < 2 else 2
                        for kt in range(first, 4):
                            last = mm(ps[B_O][e * HD:(e + 1) * HD, tt * P:(tt + 1) * P], v[:, kt, c0:c0 + HD],
                                      pt[i % 2][:, kt, :], start=kt == first, stop=kt == 3)
                        st.did(pe_step, last, *t)
                pe.wait_ge(dve_step, dv_.at("out", 7))
                down(n0 + MIX_IN[l], 4, b, NW_POST[b], None)

            pe.wait_ge(consts_in, 16)
            pe.wait_ge(rows_in, 16 * 11)
            for i, n in enumerate((P, P, 5)):
                nc.tensor.transpose(ps[i][:, 0:n], rows[0:n, i, :], ident[0:n, 0:n]).then_inc(rows_t, 1)
            pe.wait_ge(x_in, 32)
            xrow = Ysb[:, :, :].rearrange("p (t a) n -> p t (a n)", t=4)
            for i, ch in enumerate((3, 4, 5, 6, 7, 0, 1, 2)):
                if ch < 3:
                    pe.wait_ge(cols_ready, 3)
                for t in range(4):
                    last = nc.tensor.transpose(ps[ch][:, t * P:(t + 1) * P], xrow[:, t, ch * P:(ch + 1) * P], ident)
                last.then_inc(xt_done, 1)
            pe.wait_ge(x_loaded, 8)
            pre_sums(0, NT)
            pe.wait_ge(s_ready, 2)
            for i, bank in enumerate(PRO_BANKS):
                pe.wait_ge(pro_in[i], 16)
                for kk in range(KD):
                    last = mm(ps[bank][0:4, :], sT[:, kk, :], ada_pro[:, kk, i * ADA_W:(i + 1) * ADA_W],
                              start=kk == 0, stop=kk == KD - 1)
                last.then_inc(pro_mm, 1)
            for i in range(ADA_PRO):
                pe.wait_ge(pro_row, i + 1)
                for j in range(ADA_CH):
                    ch = ADA_CH * i + j
                    last = ada_fold(PRO_BANKS[0], ch, Ysb[0:4, i, j * P:(j + 1) * P])
            last.then_inc(pro_flip, 1)

            for l in range(LAYERS):
                ffn(2 * l, phase[3 * l], 3 * l, l, 0)
                pre_sums(3 * l + 1, NW_PRE[3 * l + 1])
                mixer(l, 3 * l + 1)
                pre_sums(3 * l + 2, NW_PRE[3 * l + 2])
                ffn(2 * l + 1, phase[3 * l + 2], 3 * l + 2, l, 1)
                if l + 1 < LAYERS:
                    pre_sums(3 * l + 3, NW_PRE[3 * l + 3])
            for ch in range(KD):
                pe.wait_ge(*x_landed(5, ch))
            for t in range(2):
                for half in range(2):
                    for j in range(4):
                        ch = 4 * half + j
                        last = nc.tensor.transpose(ps[2 * t + half][:, j * P:(j + 1) * P], X[:, ch, t * P:(t + 1) * P], ident)
                    last.then_inc(ot_done, 1)

        @block.scalar
        def _(act):
            A_ = nc.scalar.activation

            def copy(o, i):
                return A_(o, i, ACT.Copy)

            def split_hi(n, used, value, reg=None):
                if used is not None:
                    act.wait_ge(used, value)
                w = unit_width(n if reg is None else n + reg[1])
                act.wait_ge(w_in[n % 2], 16 * (n // 2 + 1) if reg is None else 16 * (n // 2 + reg[0] + 1))
                copy(wsp[n % 2][:, 0, 0:w], raw[n % 2][:, 0:w]).then_inc(hi_ready, 1)

            def post(b):
                w = NW_POST[b]
                for ch in range(KD):
                    act.wait_ge(y_out, KD * b + ch + 1)
                    if ch >= 2:
                        act.wait_ge(sq1_used, KD * b + ch - 1)
                    A_(T[ch % 2][:, 0:w], Ysb[:, ch, 0:w], ACT.Square).then_inc(sq1_ready, 1)
                act.wait_ge(sq1_used, KD * (b + 1))
                A_(T[2][:, 0:w], ps[SS1][:, 0:w], ACT.Sqrt, bias=epsc[:, 0:1], scale=1.0 / D).then_inc(root_ready, 1)

            def pre(r):
                w = NW_PRE[r]
                for ch in range(KD):
                    if r == 0:
                        act.wait_ge(x_loaded, 8)
                    else:
                        act.wait_ge(*x_landed(r - 1, ch))
                    if ch >= 2:
                        act.wait_ge(sq2_used, KD * r + ch - 1)
                    A_(T[ch % 2][:, 0:w], X[:, ch, 0:w], ACT.Square).then_inc(sq2_ready, 1)
                if r:
                    ada_row((ada_norm[r] + 1) * ADA_PCS, B_ADA_NORM)
                act.wait_ge(sq2_used, KD * (r + 1))
                A_(T[2][:, 0:w], ps[SS2][:, 0:w], ACT.Sqrt, bias=epsc[:, 0:1], scale=1.0 / D).then_inc(root_ready, 1)
                if r == 0:
                    for i, bank in enumerate(PRO_BANKS):
                        act.wait_ge(pro_mm, i + 1)
                        copy(Ysb[0:4, i, :], ps[bank][0:4, :]).then_inc(pro_row, 1)
                m0_ = (r // 3) * 72 + (r % 3) * 24
                if r:
                    act.wait_ge(mod_ready, ada_blocks(m0_ + 8))
                for ch in range(KD):
                    act.wait_ge(ht_ready, KD * r + ch + 1)
                    for s in range(w // LAT):
                        c_ = slice(s * LAT, (s + 1) * LAT)
                        last = A_(h_whole[:, ch, 1, c_], h_whole[:, ch, 1, c_], ACT.Identity, bias=mod[:, m0_ + ch, s:s + 1])
                    last.then_inc(hv_ready, 1)

            def ada_row(piece_count, bank):
                act.wait_ge(ada_mm, piece_count)
                copy(arow[:], ps[bank][0:4, :]).then_inc(arow_ready, 1)

            def ada_high(slot, landed, used, flipped=None):
                act.wait_ge(ada_in[slot], landed)
                if used is not None:
                    act.wait_ge(ada_mm, used)
                if flipped is not None:
                    act.wait_ge(ada_flip, flipped)
                copy(ada_hi[:], ada_raw[:, slot, :, :]).then_inc(ada_hi_ready, 1)

            def gate_up(q, n0, w):
                def steps(lo_, hi_, with_ada):
                    with act.Fori(lo_, hi_) as i:
                        for j in range(2):
                            if with_ada:
                                ada_high(1 - j, 32 * i + 16 * (j + 1), ADA_PCS * i + j + 1)
                            act.wait_ge(gate_done, q * NF + 2 * i + j + 1)
                            act.wait_ge(alo_done, q * NF + 2 * i + j + 1)
                            A_(T[j][:, 0:w], ps[j][:, 0:w], ACT.Silu).then_inc(silu_done, 1)
                        split_hi(n0 + 2, gate_done, q * NF + 2 * i + 2, reg=(i, 0))
                        if with_ada:
                            ada_high(1, 32 * i + 32, ADA_PCS * i + 3)
                        for j in range(2):
                            act.wait_ge(prod_done, q * NF + 2 * i + j + 3)
                            copy(A[:, bass.ds(2 * i + j, 1), 0, 0:w].rearrange("p a n -> p (a n)"), T[j][:, 0:w]).then_inc(ahi_done, 1)
                            if with_ada and j == 0:
                                ada_row(ADA_PCS * i + ADA_PCS, 4)
                                ada_high(0, 32 * i + 48, ADA_PCS * i + 4, i + 1)
                        split_hi(n0 + 3, up_done, q * NF + 2 * i + 2, reg=(i, 0))

                if q == 0:
                    steps(0, ADA_FFN, True)
                steps(ADA_FFN if q == 0 else 0, GU_STEPS, False)

            def down_splits(n1, units, d0, b):
                if units == DOWN_UNITS:
                    for u in range(2):
                        split_hi(n1 + u + 2, down_done, d0 + u + 1)
                    with act.Fori(1, 4) as i:
                        for j in range(2):
                            split_hi(n1 + 2 + j, down_done, d0 + 2 * i + j + 1, reg=(i, 0))
                    rest = (8, 9)
                else:
                    rest = range(units - 1)
                for u in rest:
                    if n1 + u + 2 < last_unit:
                        split_hi(n1 + u + 2, down_done, d0 + u + 1)

            def last_split(n1, units, b):
                if n1 + units + 1 < last_unit:
                    split_hi(n1 + units + 1, y_done, KD * (b + 1))

            def mixer(l, b):
                toks, items, pe, st, dv_ = plans[l]
                n0 = phase[b]
                pp, pt = probs[l], (pt0, pt1)[l]
                for t in toks:
                    k = t[0]
                    if k == "split":
                        split_hi(n0 + t[1], pe_step, pe.at(*unit_end[l][t[1] - 2]))
                    elif k in ("rank", "norm"):
                        n = 2 if t[1] == "cq" else 1
                        src = {"cq": [qh0[0], qh0[1]], "ckv": [qh0[2]], "bk": [kbuf["bk"]]}.get(t[1]) or [qh0[t[2] % 2]]
                        for i in range(n):
                            act.wait_ge(dve_step, dv_.at("proj", t[1], i if t[1] == "cq" else t[2]))
                            name = ("square", t[1], t[2], i)
                            st.did(act_step, A_(T[i][:], src[i][:], ACT.Square), *name)
                        act.wait_ge(pe_step, pe.at("sum", t[1], t[2]))
                        d_ = {"cq": 2 * P, "ckv": P}.get(t[1], HD)
                        st.did(act_step, A_(Rm[:], work_bank(l, ("sum", t[1], t[2]))[:, 0:NT], ACT.Sqrt, bias=epsc[:, 0:1], scale=1.0 / d_), "root", *t[1:])
                        if k == "rank":
                            for i in range(n):
                                act.wait_ge(dve_step, dv_.at("scaled", t[1], i))
                                dst = cqn[:, i, 0, :] if t[1] == "cq" else ckvn[:, 0, :]
                                st.did(act_step, copy(dst, src[i][:]), "hi", t[1], i)
                    elif k == "score":
                        i = t[1]
                        p, e, tt = items[i]
                        k0_ = 0 if tt < 2 else LAT
                        sink = l == 1 and i < 16
                        act.wait_ge(dve_step, dv_.at("sinkmax" if sink else "max", i))
                        if i >= DEEP:
                            act.wait_ge(pe_step, pe.at("turn", i - DEEP))
                        st.did(act_step, A_(pp[i % DEEP][:, k0_:NT], ps[B_S[i % DEEP]][:, k0_:NT], ACT.Exp, bias=nmax[:, i % DEEP:i % DEEP + 1],
                                            accum_out=psum_[:, i % DEEP:i % DEEP + 1]), "exp", i)
                        if sink:
                            st.did(act_step, A_(sexp[:, i % DEEP:i % DEEP + 1], sinkc[:, 2 * p + e:2 * p + e + 1], ACT.Exp,
                                                bias=nmax[:, i % DEEP:i % DEEP + 1]), "sinkexp", i)
                    elif k == "ada":
                        if (t[1] + 1) % ADA_PCS == 0:
                            ada_row(t[1] + 1, B_ADA)
                    elif k == "turn":
                        i = t[1]
                        a = 0 if items[i][2] < 2 else 2
                        act.wait_ge(pe_step, pe.at("turn", i))
                        if i >= 2:
                            act.wait_ge(pe_step, pe.at("value", i - 2))
                        st.did(act_step, copy(pt[i % 2][:, a:4, :].rearrange("p a n -> p (a n)"), ps[B_PT][:, a * P:NT]), "turn", i)
                    elif k == "out":
                        p = t[1]
                        w = NW_POST[b]
                        act.wait_ge(pe_step, pe.at("value", (p + 1) * (8 if l == 0 else 4) - 1))
                        st.did(act_step, copy(A[:, p, 0, 0:w], ps[B_O][:, 0:w]), "out", p)

            act.sem_inc(silu_done, 2)
            act.wait_ge(cols_ready, 3)
            for s, c0 in ((0, C_C), (1, C_CC)):
                A_(sT[:, :, s], cols[:, c0:c0 + KD], ACT.Silu).then_inc(s_ready, 1)
            act.wait_ge(s_ready, 2)
            copy(sS[:, :, 0:2], sT[:, :, 0:2]).then_inc(s_split, 1)
            act.wait_ge(zero_ready, 1)
            pre(0)
            ada_high(0, 16, None)
            split_hi(0, None, 0)
            split_hi(1, None, 0)
            for l in range(LAYERS):
                d0 = l * (2 * (DOWN_UNITS - 1) + 3)
                gate_up(2 * l, phase[3 * l], NW_PRE[3 * l])
                down_splits(phase[3 * l] + 2 * GU_STEPS, DOWN_UNITS, d0, 3 * l)
                post(3 * l)
                last_split(phase[3 * l] + 2 * GU_STEPS, DOWN_UNITS, 3 * l)
                pre(3 * l + 1)
                mixer(l, 3 * l + 1)
                down_splits(phase[3 * l + 1] + MIX_IN[l], 4, d0 + DOWN_UNITS - 1, 3 * l + 1)
                post(3 * l + 1)
                last_split(phase[3 * l + 1] + MIX_IN[l], 4, 3 * l + 1)
                pre(3 * l + 2)
                gate_up(2 * l + 1, phase[3 * l + 2], NW_PRE[3 * l + 2])
                down_splits(phase[3 * l + 2] + 2 * GU_STEPS, DOWN_UNITS, d0 + DOWN_UNITS - 1 + 3, 3 * l + 2)
                post(3 * l + 2)
                last_split(phase[3 * l + 2] + 2 * GU_STEPS, DOWN_UNITS, 3 * l + 2)
                if l + 1 < LAYERS:
                    pre(3 * l + 3)

        @block.vector
        def _(dve):
            TT, STT, TS = nc.vector.tensor_tensor, nc.vector.scalar_tensor_tensor, nc.vector.tensor_scalar
            gains = [0]

            def split_lo(n, reg=None):
                w = unit_width(n)
                dve.wait_ge(hi_ready, n + 1 if reg is None else reg + 1)
                TT(wsp[n % 2][:, 1, 0:w], raw[n % 2][:, 0:w], wsp[n % 2][:, 0, 0:w].bitcast(F32), ALU.subtract).then_inc(lo_ready, 1)

            def ada_low(slot, count):
                dve.wait_ge(ada_hi_ready, count)
                TT(ada_lo[:, slot, :, :], ada_raw[:, slot, :, :], ada_hi[:].bitcast(F32), ALU.subtract).then_inc(ada_lo_ready, 1)

            def ada_out(block, bank):
                dve.wait_ge(ada_flip, block + 1)
                m = bass.ds((ADA_PRO + block) * ADA_CH, ADA_CH)
                bias = cols[:, m].rearrange("p (a b) -> p a b", b=1).broadcast_to([P, ADA_CH, 2])
                got = ps[bank][:, 0:2 * ADA_CH].rearrange("p (a b) -> p a b", b=2)
                TT(mod[:, m, :], got, bias, ALU.add).then_inc(mod_ready, 1)

            def norm_cols(l, i):
                g = cols[:, C_NORM + l * 48 + i * 8:C_NORM + l * 48 + i * 8 + 8]
                return g.rearrange("p (a b) -> p a b", b=1).broadcast_to([P, KD, 2])

            def invert(count, w):
                dve.wait_ge(root_ready, count)
                nc.vector.reciprocal(R[:, 0:w], T[2][:, 0:w]).then_inc(inv_ready, 1)
                dve.wait_ge(inv_ready, count)

            def gain(ins):
                gains[0] += 1
                ins.then_inc(gain_ready, 1)

            def post(b, inv):
                w = NW_POST[b]
                l, slot = b // 3, b % 3
                m0_ = l * 72 + slot * 24 + 16
                dve.wait_ge(mod_ready, ada_blocks(m0_ + 8))
                gain(STT(gcol[:], mod[:, m0_:m0_ + 8, :], 1.0 if slot == 1 else 0.5, norm_cols(l, 2 * slot + 1), ALU.mult, ALU.mult))
                for ch in range(KD):
                    dve.wait_ge(y_done, KD * b + ch + 1)
                    nc.vector.tensor_copy(Ysb[:, ch, 0:w], ps[bank_of(ch)][:, 0:w]).then_inc(y_out, 1)
                dve.wait_ge(gain_ready, gains[0])
                invert(inv, w)
                for ch in range(KD):
                    for s in range(w // LAT):
                        c_ = slice(s * LAT, (s + 1) * LAT)
                        last = STT(Ysb[:, ch, c_], Ysb[:, ch, c_], gcol[:, ch, s:s + 1], R[:, c_], ALU.mult, ALU.mult)
                    last.then_inc(upd_ready, 1)
                dve.wait_ge(upd_ready, KD * (b + 1))
                for ch in range(POOL_CH, KD):
                    TT(X[:, ch, 0:w], X[:, ch, 0:w], Ysb[:, ch, 0:w], ALU.add).then_inc(xd_ready, 1)

            def pre(r, inv):
                w = NW_PRE[r]
                l, slot = r // 3, r % 3
                m0_ = l * 72 + slot * 24
                if r:
                    ada_out(ada_norm[r], B_ADA_NORM)
                    dve.wait_ge(mod_ready, ada_norm[r] + 2)
                gain(STT(scol[:], mod[:, m0_ + 8:m0_ + 16, :], 1.0, norm_cols(l, 2 * slot), ALU.add, ALU.mult))
                dve.wait_ge(gain_ready, gains[0])
                if inv is not None:
                    invert(inv, w)

                def high(ch):
                    dve.wait_ge(hv_ready, KD * r + ch + 1)
                    nc.vector.tensor_copy(H[:, ch, 0, 0:w], h_whole[:, ch, 1, 0:w]).then_inc(hh_ready, 1)

                for ch in range(KD):
                    for s in range(w // LAT):
                        c_ = slice(s * LAT, (s + 1) * LAT)
                        last = STT(h_whole[:, ch, 1, c_], X[:, ch, c_], scol[:, ch, s:s + 1], R[:, c_], ALU.mult, ALU.mult)
                    last.then_inc(ht_ready, 1)
                    if ch >= 2:
                        high(ch - 2)
                high(KD - 2)
                high(KD - 1)

            def gate_up(q, n0, w, l, s):
                def steps(lo_, hi_, with_ada):
                    with dve.Fori(lo_, hi_) as i:
                        if with_ada:
                            ada_low(1, ADA_PCS * i + 2)
                            ada_low(0, ADA_PCS * i + 3)
                        split_lo(n0 + 2, n0 + 2 + 2 * i)
                        if with_ada:
                            ada_low(1, ADA_PCS * i + 4)
                        for j in range(2):
                            dve.wait_ge(up_done, q * NF + 2 * i + j + 1)
                            dve.wait_ge(silu_done, q * NF + 2 * i + j + 3)
                            TT(T[j][:, 0:w], ps[2 + j][:, 0:w], T[j][:, 0:w], ALU.mult).then_inc(prod_done, 1)
                        if with_ada:
                            ada_out(i, 4)
                            ada_low(0, ADA_PCS * i + 5)
                        for j in range(2):
                            dve.wait_ge(ahi_done, q * NF + 2 * i + j + 1)
                            o = A[:, bass.ds(2 * i + j, 1), 1, 0:w].rearrange("p a n -> p (a n)")
                            hi = A[:, bass.ds(2 * i + j, 1), 0, 0:w].rearrange("p a n -> p (a n)")
                            TT(o, T[j][:, 0:w], hi.bitcast(F32), ALU.subtract).then_inc(alo_done, 1)
                        split_lo(n0 + 3, n0 + 3 + 2 * i)

                if q == 0:
                    steps(0, ADA_FFN, True)
                steps(ADA_FFN if q == 0 else 0, GU_STEPS, False)

            def down_splits(n1, units):
                if units == DOWN_UNITS:
                    for u in range(2):
                        split_lo(n1 + u + 2)
                    with dve.Fori(1, 4) as i:
                        for j in range(2):
                            split_lo(n1 + 2 + j, n1 + 2 + j + 2 * i)
                    rest = (8, 9)
                else:
                    rest = range(units - 1)
                for u in rest:
                    if n1 + u + 2 < last_unit:
                        split_lo(n1 + u + 2)

            def last_split(n1, units):
                if n1 + units + 1 < last_unit:
                    split_lo(n1 + units + 1)

            def mixer(l, b):
                toks, items, pe, ac, st = plans[l]
                n0 = phase[b]
                mc = (mc0, mc1)[l]
                qh, kh, pp = (qh0, kh0, probs[0]) if l == 0 else (qh1, None, probs[1])
                kd_ = (kdup0, kdup1)[l]
                tiles = 4 if l == 0 else 2
                dve.wait_ge(mix_in, 16 * (l + 1))
                dve.wait_ge(sink_in, 16)
                if l == 1:
                    dve.wait_ge(toe_ready, 8)
                for t in toks:
                    k = t[0]
                    if k == "split":
                        split_lo(n0 + t[1])
                    elif k == "flip":
                        ada_out(t[1], B_ADA)
                    elif k == "proj":
                        o = work_bank(l, t)
                        what, j = t[1:]
                        dve.wait_ge(pe_step, pe.at(*t))
                        if what == "q":
                            if j >= 4:
                                dve.wait_ge(pe_step, pe.at("score", (j // 2 - 1) * 8 - 1))
                            last = TS(qh[j % 4][0:QK, :], o[0:QK, :], MLA_SCALE, None, ALU.mult)
                        elif what == "k":
                            if j >= 4:
                                dve.wait_ge(pe_step, pe.at("score", (j // 2 - 1) * 8 - 1))
                            last = nc.vector.tensor_copy(kh[j % 4][0:HD, :], o[0:HD, :])
                        elif (l, what) == (0, "cq"):
                            last = nc.vector.tensor_copy(qh[j][:], o[:])
                        elif what == "ckv":
                            last = nc.vector.tensor_copy(qh[2][:], o[:])
                        elif what == "kr":
                            nc.vector.memset(T[3][0:HD, 0:LAT], 0.0)
                            last = nc.vector.tensor_copy(T[3][HD:QK, :], o[0:32, :])
                        elif what == "va":
                            last = nc.vector.tensor_copy(va[:, j, :], o[:])
                        elif what in ("bk", "ck"):
                            if what == "bk":
                                dve.wait_ge(pe_step, pe.at("score", 8 * 3 - 1))
                            last = nc.vector.tensor_copy(kbuf[what][:], o[:])
                        elif what in ("bv", "cv"):
                            last = nc.vector.tensor_copy((vb if l == 0 else cv)[:, :, :].rearrange("p a n -> p (a n)"), o[:])
                        elif what == "bq":
                            if j == 4 or j == 5:
                                dve.wait_ge(pe_step, pe.at("score", 8 * 4 - 1) if j == 5 else pe.at("score", 8 * 3 - 1))
                            else:
                                dve.wait_ge(pe_step, pe.at("score", (j - 1) * 8 - 1))
                            last = nc.vector.tensor_copy(qh[j % 2][:], o[:])
                        elif what == "dv":
                            u, half = j // 2, j % 2
                            last = nc.vector.tensor_copy(dv[:, 2 * half:2 * half + 2, u * 256:(u + 1) * 256],
                                                         o[:].rearrange("p (a n) -> p a n", a=2))
                        elif what == "dk":
                            last = nc.vector.tensor_copy(dk[:, j, :], o[:])
                        else:
                            if j >= 2:
                                dve.wait_ge(pe_step, pe.at("score", (j - 1) * 4 - 1))
                            last = TS(qh[j % 2][:], o[:, 0:LAT], HD_SCALE, None, ALU.mult)
                        st.did(dve_step, last, *t)
                    elif k in ("rank", "norm"):
                        what, j = t[1:]
                        n = 2 if what == "cq" else 1
                        dve.wait_ge(act_step, ac.at("root", what, j))
                        st.did(dve_step, nc.vector.reciprocal(Rm[:], Rm[:]), "inv", what, j)
                        dve.wait_ge(dve_step, st.at("inv", what, j))
                        if k == "norm":
                            src = kbuf.get(what, qh[j % 2])
                            g = cols[:, C_GK:C_GK + 1] if what == "bk" else cols[:, C_GQ:C_GQ + 1]
                            st.did(dve_step, STT(src[:], src[:], g, Rm[:], ALU.mult, ALU.mult), "normed", what, j)
                        else:
                            src = [qh[0], qh[1]] if what == "cq" else [qh[2]]
                            g0 = C_QN if what == "cq" else C_KVN
                            for i in range(n):
                                st.did(dve_step, STT(src[i][:], src[i][:], cols[:, g0 + i:g0 + i + 1], Rm[:], ALU.mult, ALU.mult),
                                       "scaled", what, i)
                            for i in range(n):
                                hi, lo_ = (cqn[:, i, 0, :], cqn[:, i, 1, :]) if what == "cq" else (ckvn[:, 0, :], ckvn[:, 1, :])
                                dve.wait_ge(act_step, ac.at("hi", what, i))
                                st.did(dve_step, TT(lo_, src[i][:], hi.bitcast(F32), ALU.subtract), "lo", what, i)
                    elif k == "rope":
                        what, j = t[1:]
                        if what in ("q", "kr"):
                            g, cc, ss = slice(HD, QK), M_C96, M_S96
                            tgt = qh[j % 4] if what == "q" else T[3]
                        else:
                            g, cc, ss = slice(0, P), M_C64, M_S64
                            tgt = kbuf.get(what, qh[j % 2])
                        dve.wait_ge(pe_step, pe.at(*t))
                        st.did(dve_step, TT(T[0][g, 0:LAT], work_bank(l, t)[g, 0:LAT], mc[g, ss:ss + LAT], ALU.mult), "sin", what, j)
                        st.did(dve_step, TT(T[1][g, 0:LAT], tgt[g, 0:LAT], mc[g, cc:cc + LAT], ALU.mult), "cos", what, j)
                        dve.wait_ge(dve_step, st.at("cos", what, j))
                        st.did(dve_step, TT(tgt[g, 0:LAT], T[0][g, 0:LAT], T[1][g, 0:LAT], ALU.add), *t)
                    elif k == "dup":
                        dve.wait_ge(dve_step, st.at("rope", *t[1:]))
                        if t[1] == "kr":
                            for i in range(4):
                                last = nc.vector.tensor_copy(kh[i][HD:QK, :], T[3][HD:QK, :])
                        else:
                            for g in range(2):
                                for half in range(2):
                                    last = nc.vector.tensor_copy(kd_[g][half * HD:(half + 1) * HD, :], kbuf[t[1]][g * HD:(g + 1) * HD, :])
                        st.did(dve_step, last, *t)
                    elif k == "score":
                        i = t[1]
                        p, e, tt = items[i]
                        k0_ = 0 if tt < 2 else LAT
                        S = ps[B_S[i % DEEP]]
                        dve.wait_ge(pe_step, pe.at(*t))
                        if l == 1:
                            bias = mc[:, M_SWA + tt * LAT:M_SWA + (tt + 1) * LAT] if p < 4 else \
                                toe[:, 2 * (p - 4) + e, 2 - 2 * tt + 0:6 - 2 * tt, :].rearrange("p a n -> p (a n)")
                            st.did(dve_step, TT(S[:, 0:LAT], S[:, 0:LAT], bias, ALU.add), "bias", i)
                            dve.wait_ge(dve_step, st.at("bias", i))
                        if i >= DEEP:
                            dve.wait_ge(act_step, ac.at("sinkexp" if l == 1 and i - DEEP < 16 else "exp", i - DEEP))
                        sink = l == 1 and i < 16
                        if sink:
                            m = smax[:, i % DEEP:i % DEEP + 1]
                            st.did(dve_step, nc.vector.tensor_reduce(m, S[:, k0_:NT], AX_X, ALU.max), "max", i)
                            dve.wait_ge(dve_step, st.at("max", i))
                            st.did(dve_step, TS(nmax[:, i % DEEP:i % DEEP + 1], m, sinkc[:, 2 * p + e:2 * p + e + 1], -1.0, ALU.max, ALU.mult),
                                   "sinkmax", i)
                        else:
                            st.did(dve_step, nc.vector.tensor_reduce(nmax[:, i % DEEP:i % DEEP + 1], S[:, k0_:NT], AX_X, ALU.max, negate=True),
                                   "max", i)
                    elif k == "prob":
                        i = t[1]
                        k0_ = 0 if items[i][2] < 2 else LAT
                        tot = psum_[:, i % DEEP:i % DEEP + 1]
                        if l == 1 and i < 16:
                            dve.wait_ge(act_step, ac.at("sinkexp", i))
                            st.did(dve_step, TT(smax[:, i % DEEP:i % DEEP + 1], tot, sexp[:, i % DEEP:i % DEEP + 1], ALU.add), "total", i)
                            dve.wait_ge(dve_step, st.at("total", i))
                            tot = smax[:, i % DEEP:i % DEEP + 1]
                        else:
                            dve.wait_ge(act_step, ac.at("exp", i))
                        st.did(dve_step, nc.vector.reciprocal(pinv[:, i % DEEP:i % DEEP + 1], tot), "inv", i)
                        dve.wait_ge(dve_step, st.at("inv", i))
                        st.did(dve_step, TS(pp[i % DEEP][:, k0_:NT], pp[i % DEEP][:, k0_:NT], pinv[:, i % DEEP:i % DEEP + 1], None, ALU.mult), "prob", i)
                    elif k == "out":
                        p = t[1]
                        w = NW_POST[b]
                        dve.wait_ge(act_step, ac.at("out", p))
                        st.did(dve_step, TT(A[:, p, 1, 0:w], ps[B_O][:, 0:w], A[:, p, 0, 0:w].bitcast(F32), ALU.subtract), "out", p)

            nc.vector.memset(sT[:, :, 2:4], 0.0)
            nc.vector.memset(epsc[:], EPS).then_inc(zero_ready, 1)
            dve.sem_inc(prod_done, 2)
            dve.sem_inc(alo_done, 2)
            for i, (c0, n) in enumerate(((0, P), (P, P), (2 * P, 5))):
                dve.wait_ge(rows_t, i + 1)
                nc.vector.tensor_copy(cols[:, c0:c0 + n], ps[i][:, 0:n]).then_inc(cols_ready, 1)
            dve.wait_ge(cols_ready, 3)
            gain(TS(cols[:, C_GQ:C_GQ + 1], cols[:, C_GQ:C_GQ + 1], HD_SCALE, None, ALU.mult))
            dve.wait_ge(consts_in, 16)
            TT(fold[:], ident[0:4, 0:2], ident[0:4, 2:4], ALU.add)
            dve.wait_ge(s_split, 1)
            TT(sS[:, :, 2:4], sT[:, :, 0:2], sS[:, :, 0:2].bitcast(F32), ALU.subtract).then_inc(s_split, 1)
            for i, ch in enumerate((3, 4, 5, 6, 7, 0, 1, 2)):
                dve.wait_ge(xt_done, i + 1)
                nc.vector.tensor_copy(X[:, ch, :], ps[ch][:]).then_inc(x_loaded, 1)
            invert(1, NT)
            dve.wait_ge(pro_flip, 1)
            n = ADA_PRO * ADA_CH
            bias = cols[:, 0:n].rearrange("p (a b) -> p a b", b=1).broadcast_to([P, n, 2])
            got = ps[PRO_BANKS[0]][:, 0:2 * n].rearrange("p (a b) -> p a b", b=2)
            TT(mod[:, 0:n, :], got, bias, ALU.add).then_inc(mod_ready, 1)
            dve.wait_ge(mod_ready, 1)
            pre(0, None)
            ada_low(0, 1)
            split_lo(0)
            split_lo(1)
            for l in range(LAYERS):
                for s in range(2):
                    b = 3 * l + 2 * s
                    gate_up(2 * l + s, phase[b], NW_PRE[b], l, s)
                    n1 = phase[b] + 2 * GU_STEPS
                    down_splits(n1, DOWN_UNITS)
                    post(b, 2 * b + 2)
                    last_split(n1, DOWN_UNITS)
                    if b < 5:
                        pre(b + 1, 2 * b + 3)
                    if s == 0:
                        mixer(l, b + 1)
                        n1 = phase[b + 1] + MIX_IN[l]
                        down_splits(n1, 4)
                        post(b + 1, 2 * b + 4)
                        last_split(n1, 4)
                        pre(b + 2, 2 * b + 5)
            for i in range(4):
                dve.wait_ge(ot_done, i + 1)
                t, half = i // 2, i % 2
                nc.vector.tensor_copy(outs[:, t, half * 512:(half + 1) * 512], ps[i][:]).then_inc(o_ready, 1)


_INS = ['x', 'c', 'ctx', 'c_ctx', 'ada_w', 'ada_b', 'norm_g', 'ffn_w_gate', 'ffn_w_up', 'ffn_w_down',
        'ab_w_in', 'mla_q_norm', 'mla_w_uq', 'mla_kv_norm', 'mla_w_ukv', 'gqa_q_norm', 'gqa_k_norm',
        'ab_w_out', 'cd_w_in', 'swa_sink', 'na_rpb', 'cd_w_out']


def kernel(**inputs):
    import numpy as _np
    import concourse.bacc as _bacc
    from concourse import mybir as _mybir
    from concourse.bass_utils import run_bass_kernel_spmd as _run

    nc = _bacc.Bacc("TRN2", target_bir_lowering=False, num_devices=1)
    arrays, args = {}, []
    for name in _INS:
        a = _np.ascontiguousarray(inputs[name])
        arrays[f"in_{name}"] = a
        args.append(nc.dram_tensor(f"in_{name}", a.shape, _mybir.dt.from_np(a.dtype), kind="ExternalInput").ap())
    k = constants()
    arrays["in_consts"] = k
    args.append(nc.dram_tensor("in_consts", k.shape, _mybir.dt.float32, kind="ExternalInput").ap())
    args.append(nc.dram_tensor("out_0", (1, LAT, D), _mybir.dt.float32, kind="ExternalOutput").ap())
    dit_kernel(nc, *args)
    r = _run(nc, [arrays], core_ids=[0])
    return r.results[0]["out_0"]
```

```python
import concourse.bass as bass
from concourse import mybir
from contextlib import ExitStack
import numpy as np

F32 = mybir.dt.float32
F32R = mybir.dt.float32r
ALU = mybir.AluOpType
ACT = mybir.ActivationFunctionType
AX_X = mybir.AxisListType.X

P = 128
D = 1024
KD = D // P
LAT = 256
CTX = 256
NT = LAT + CTX
DFF = 2816
NF = DFF // P
LAYERS = 2
EPS = 1e-6
UW = 2048
UF = UW // KD
GU_STEPS = DFF // UF
DOWN_UNITS = NF * D // UW
ADA_W = 512
ADA_CH = ADA_W // P
ADA_K = 2
ADA_PCS = KD // ADA_K
ADA_PRO = 4
ADA_ALL = LAYERS * 9 * D // ADA_W
ADA_FFN = 7
ADA_MIX = (15, 5)
DEEP = 3
POOL_CH = 6
HD = 64
QK = 96
MLA_SCALE = float(QK) ** -0.5
HD_SCALE = float(HD) ** -0.5
GRID = 64
NEG = -1e30

C_ADAB, C_NORM, C_C, C_CC, C_QN, C_KVN, C_GQ, C_GK = 0, 144, 240, 248, 256, 258, 259, 260
N_COLS = 264

K_ID, K_ONE, K_KEEP = 0, 128, 256
M_BLK, M_P64, M_P96, M_C64, M_S64, M_C96, M_S96, M_END0 = 0, 128, 256, 384, 640, 896, 1152, 1408
M_SWA, M_NA, M_END1 = 1408, 1920, 1984


def constants():
    k = np.zeros((P, K_KEEP + M_END1), np.float32)
    k[:, K_ID:K_ID + P] = np.eye(P)
    k[:, K_ONE:K_ONE + P] = 1.0
    m = k[:, K_KEEP:]
    blk = np.arange(P) // HD
    m[:, M_BLK:M_BLK + P] = blk[:, None] == blk[None, :]
    for o in range(P):
        first = o % HD < HD // 2
        m[o + 32 if first else o - 32, M_P64 + o] = -1.0 if first else 1.0
    for o in range(64, QK):
        first = o < 80
        m[o + 16 if first else o - 16, M_P96 + o] = -1.0 if first else 1.0
    tok = np.arange(LAT)
    row, col = (tok // GRID).astype(np.float32), (tok % GRID).astype(np.float32)

    def angles(rot):
        per_axis = rot // 2
        inv = np.float32(10000.0) ** (-np.arange(0, per_axis, 2, dtype=np.float32) / np.float32(per_axis))
        return np.concatenate([row[:, None] * inv, col[:, None] * inv], -1).astype(np.float32)

    a64, a32 = angles(HD).T, angles(32).T
    m[:, M_C64:M_C64 + LAT] = np.cos(a64)[np.arange(P) % 32]
    m[:, M_S64:M_S64 + LAT] = np.sin(a64)[np.arange(P) % 32]
    m[64:QK, M_C96:M_C96 + LAT] = np.cos(a32)[np.arange(32) % 16]
    m[64:QK, M_S96:M_S96 + LAT] = np.sin(a32)[np.arange(32) % 16]
    for t in range(2):
        far = np.abs((t * P + np.arange(P))[:, None] - tok[None, :]) > 128
        m[:, M_SWA + t * LAT:M_SWA + (t + 1) * LAT] = np.where(far, NEG, 0.0)
    qc = np.arange(P) % GRID
    c0 = np.clip(qc - 8, 0, GRID - 16)
    kc = np.arange(GRID)
    m[:, M_NA:M_NA + GRID] = np.where((kc[None] >= c0[:, None]) & (kc[None] < c0[:, None] + 16), 0.0, NEG)
    return k


class Steps:

    def __init__(self, names, base):
        self.value = {n: base + i + 1 for i, n in enumerate(names)}
        self.next = base
        self.end = base + len(names)

    def at(self, *name):
        return self.value[name]

    def did(self, sem, instruction, *name):
        self.next += 1
        assert self.value[name] == self.next, name
        instruction.then_inc(sem, 1)



def mixer_tokens(layer, block):
    tok = []
    tiles = 4 if layer == 0 else 2
    items = [(p, e, t) for p in range(8) for e in range(2) for t in range(tiles)]

    def prep(p):
        if layer == 0 and p < 4:
            out = []
            for e in range(2):
                out += [("proj", "q", 2 * p + e), ("proj", "k", 2 * p + e), ("rope", "q", 2 * p + e)]
            if p == 3:
                out += [("split", 4), ("split", 5)]
            return out
        out = []
        if layer == 0:
            if p == 4:
                out += [("proj", "bk", 0), ("norm", "bk", 0), ("rope", "bk", 0), ("dup", "bk", 0),
                        ("proj", "bv", 0), ("turnv", "bv", 0), ("split", 6)]
            out += [("proj", "bq", p), ("norm", "bq", p), ("rope", "bq", p)]
            if p == 5:
                out += [("split", 7)]
            if p == 7:
                out += [("split", 8)]
            return out
        cq, dq = [("proj", "cq", p), ("rope", "cq", p)], [("proj", "dq", p)]
        dv, dk = [("proj", "dv", j) for j in range(4)], [("proj", "dk", j) for j in range(4)]
        return [cq,
                cq + [("split", 3), dv[0]],
                [dv[1], ("split", 4), dv[2], dv[3], ("split", 5)] + cq,
                cq + [("split", 6), dk[0], dk[1], ("split", 7)],
                [dk[2], dk[3], ("split", 8)] + dq,
                dq + [("split", 9)],
                dq,
                dq + [("split", 10)]][p]

    if layer == 0:
        tok += [("proj", "cq", 0), ("proj", "cq", 1), ("split", 2), ("proj", "ckv", 0), ("proj", "kr", 0),
                ("split", 3), ("rank", "cq", 0), ("ada", block * ADA_PCS), ("ada", block * ADA_PCS + 1),
                ("rank", "ckv", 0), ("rope", "kr", 0), ("dup", "kr", 0)]
        tok += [("ada", block * ADA_PCS + j) for j in range(2, ADA_PCS)]
        tok += [("proj", "va", t) for t in range(4)]
        tok += [("flip", block)]
    else:
        tok += [("proj", "ck", 0), ("rope", "ck", 0), ("dup", "ck", 0), ("proj", "cv", 0), ("split", 2), ("turnv", "cv", 0)]
    tok += prep(0)
    tok += [("score", 0), ("score", 1)]
    per_pair = 2 * tiles
    waiting, flip = prep(1), None
    pieces = ADA_MIX[layer] * ADA_PCS
    pieces0 = extra = ADA_PCS if layer == 0 else 0
    for i in range(len(items) + 1):
        if i < len(items):
            if i % per_pair == per_pair - 1:
                waiting = prep(i // per_pair + 2) if i // per_pair + 2 < 8 else []
            tok.append(("prob", i))
            if flip is not None:
                tok.append(("flip", flip))
                flip = None
            left = (per_pair - 2 - i) % per_pair + 1
            for _ in range(-(-len(waiting) // left)):
                tok.append(waiting.pop(0))
            while flip is None and extra < min(pieces, pieces0 + -(-(i + 1) * (pieces - pieces0) // (len(items) - 8))):
                tok.append(("ada", block * ADA_PCS + extra))
                extra += 1
                if extra % ADA_PCS == 0:
                    flip = block + extra // ADA_PCS - 1
            if i + 2 < len(items):
                tok.append(("score", i + 2))
            tok.append(("turn", i))
        if i >= 1:
            tok.append(("value", i - 1))
            p, e, t = items[i - 1]
            if e == 1 and t == tiles - 1:
                tok.append(("out", p))
    if flip is not None:
        tok.append(("flip", flip))
    assert extra == pieces
    return tok, items


def pe_steps(t, layer):
    k = t[0]
    if k == "rank":
        return [("sum",) + t[1:]]
    if k == "norm":
        return [("sum",) + t[1:]]
    if k in ("proj", "turnv", "rope", "score", "turn", "value"):
        return [t]
    return []


def act_steps(t, layer):
    k = t[0]
    if k == "proj" and t[1] == "bq":
        return [("square",) + t[1:] + (0,)]
    if k == "norm" and t[1] == "bq":
        return []
    if k in ("rank", "norm"):
        n = 2 if t[1] == "cq" else 1
        out = [("square", t[1], t[2], c) for c in range(n)] + [("root",) + t[1:]]
        if k == "rank":
            out += [("hi", t[1], c) for c in range(n)]
        return out
    if k == "score":
        return [("exp", t[1])] + ([("sinkexp", t[1])] if layer == 1 and t[1] < 16 else [])
    if k == "turn":
        return [t]
    if k == "out":
        return [t]
    return []


def dve_steps(t, layer):
    k = t[0]
    if k in ("proj", "turnv"):
        return [t]
    if k == "rank":
        n = 2 if t[1] == "cq" else 1
        return [("inv",) + t[1:]] + [("scaled", t[1], c) for c in range(n)] + [("lo", t[1], c) for c in range(n)]
    if k == "norm" and t[1] == "bq":
        return [("squares",) + t[1:]]
    if k == "norm":
        return [("inv",) + t[1:], ("normed",) + t[1:]]
    if k == "rope":
        return [("sin",) + t[1:], ("cos",) + t[1:], t]
    if k == "dup":
        return [t]
    if k == "score":
        out = [("bias", t[1])] if layer == 1 else []
        out += [("max", t[1])]
        if layer == 1 and t[1] < 16:
            out += [("sinkmax", t[1])]
        if layer == 0 and t[1] >= 32:
            out += [("scaledmax", t[1])]
        return out
    if k == "prob":
        out = [("total", t[1])] if layer == 1 and t[1] < 16 else []
        return out + [("inv", t[1]), ("prob", t[1])]
    if k == "out":
        return [t]
    return []


def dit_kernel(nc, x, c, ctx_x, c_ctx, ada_w, ada_b, norm_g, ffn_w_gate, ffn_w_up, ffn_w_down,
               ab_w_in, mla_q_norm, mla_w_uq, mla_kv_norm, mla_w_ukv, gqa_q_norm, gqa_k_norm,
               ab_w_out, cd_w_in, swa_sink, na_rpb, cd_w_out, consts, out):
    es = ExitStack()
    with es:
        def sb(name, shape, dt=F32):
            return es.enter_context(nc.sbuf_tensor(name, shape, dt))

        def sem(name):
            return es.enter_context(nc.semaphore(name))

        X = sb("X", [P, KD, NT])
        raw = [sb(f"raw{s}", [P, UW]) for s in range(2)]
        wsp = [sb(f"wsp{s}", [P, 2, UW], F32R) for s in range(2)]
        with nc.sbuf_tensor("ada_raw", [P, 2, ADA_K, ADA_W], F32) as ada_raw:
            pass
        ada_lo = sb("ada_lo", [P, 2, ADA_K, ADA_W], F32R)
        with nc.sbuf_tensor("arow", [4, ADA_W], F32) as arow:
            pass
        ada_hi = sb("ada_hi", [P, ADA_K, ADA_W], F32R)
        T = [sb(f"T{i}", [P, NT]) for i in range(4)]
        cst = sb("cst", [P, K_KEEP])
        cols = sb("cols", [P, N_COLS])
        mod = sb("mod", [P, LAYERS * 72, 2])
        sT = sb("sT", [P, KD, 4])
        sS = sb("sS", [P, KD, 4], F32R)
        fold = sb("fold", [4, 2])
        gcol = sb("gcol", [P, KD, 2])
        scol = sb("scol", [P, KD, 2])
        epsc = sb("epsc", [P, 1])
        rcol = T[3][:, 0:NT // P]
        rinv = T[3][:, NT // P:2 * (NT // P)]
        spare = sb("spare", [P, 1])
        nmax = sb("nmax", [P, DEEP])
        psum_ = sb("psum_", [P, DEEP])
        pinv = sb("pinv", [P, DEEP])
        smax = sb("smax", [P, DEEP])
        sexp = sb("sexp", [P, DEEP])
        sinkc = sb("sinkc", [P, 8])
        ident, ones = cst[:, K_ID:K_ID + P], cst[:, K_ONE:K_ONE + P]

        with nc.sbuf_tensor("Ysb", [P, KD, NT], F32) as Ysb:
            pass
        with nc.sbuf_tensor("h_whole", [P, KD, 2, NT], F32) as h_whole:
            pass
        H = sb("H", [P, KD, 2, NT], F32R)
        with nc.sbuf_tensor("ada_pro", [P, KD, ADA_PRO * ADA_W], F32) as ada_pro:
            pass
        with ExitStack() as pro:
            pro_lo = pro.enter_context(nc.sbuf_tensor("pro_lo", [P, KD, ADA_PRO * ADA_W], F32R))
            pro_hi = pro.enter_context(nc.sbuf_tensor("pro_hi", [P, KD, ADA_W], F32R))
        with ExitStack() as m0:
            def sm(name, shape, dt=F32):
                return m0.enter_context(nc.sbuf_tensor(name, shape, dt))
            sm("keep0", [P, KD, 2, NT])
            mc0 = sm("mc0", [P, M_END0])
            kdup0 = [sm(f"kdup0{g}", [P, NT]) for g in range(2)]
            va = sm("va", [P, 4, 512])
            vb = sm("vb", [P, 4, P])
            cqn = sm("cqn", [P, 2, 2, NT], F32R)
            ckvn = sm("ckvn", [P, 2, NT], F32R)
            qh0 = [sm(f"qh0{i}", [P, NT]) for i in range(4)]
            kh0 = [sm(f"kh0{i}", [P, NT]) for i in range(4)]
            p0 = sm("p0", [P, NT])
            Rm = sm("Rm", [P, NT])
            ssq = sm("ssq", [P, 2, 8])
            rq = sm("rq", [P, 2, 8])
            mhalf = sm("mhalf", [P, 8])
            pt0 = [sm(f"pt0{i}", [P, 4, P]) for i in range(2)]
        with ExitStack() as m1:
            def sm(name, shape, dt=F32):
                return m1.enter_context(nc.sbuf_tensor(name, shape, dt))
            sm("keep1", [P, KD, 2, NT])
            mc1 = sm("mc1", [P, M_END1])
            toe = sm("toe", [P, 8, 6, GRID])
            kdup1 = [sm(f"kdup1{g}", [P, NT]) for g in range(2)]
            dk = sm("dk", [P, 4, NT])
            dv = sm("dv", [P, 4, 512])
            cv = sm("cv", [P, 4, P])
            qh1 = [sm(f"qh1{i}", [P, LAT]) for i in range(2)]
            p1 = [sm(f"p1{i}", [P, NT]) for i in range(2)]
            pt1 = [sm(f"pt1{i}", [P, 4, P]) for i in range(2)]
        A = sb("A", [P, NF, 2, NT], F32R)
        probs = ([p0, T[2], T[3]], p1 + [T[2]])
        vbuf = {"bv": kh0[1], "cv": dk[:, 3, :]}
        kbuf = {"bk": kh0[0], "ck": T[3]}
        pro_his = [pro_hi, wsp[1][:, :, :].rearrange("p h (k n) -> p (h k) n", n=ADA_W)]
        rows = T[0][:, 0:3 * P].rearrange("p (a b) -> p a b", a=3)
        outs = Ysb[:, 0:4, :].rearrange("p (t a) n -> p t (a n)", t=2)

        ps = [es.enter_context(nc.psum_tensor(f"ps{b}", [P, 512], F32)) for b in range(8)]
        rpb_win = nc.dram_tensor("rpb_win", (8, 7, GRID, 127), F32).ap()

        consts_in = sem("consts_in")
        rows_in = sem("rows_in")
        x_in = sem("x_in")
        pro_in = [sem(f"pro_in{i}") for i in range(4)]
        w_in = [sem(f"w_in{s}") for s in range(2)]
        hi_ready = sem("hi_ready")
        lo_ready = sem("lo_ready")
        ada_in = [sem(f"ada_in{s}") for s in range(2)]
        ada_hi_ready = sem("ada_hi_ready")
        ada_lo_ready = sem("ada_lo_ready")
        ada_mm = sem("ada_mm")
        arow_ready = sem("arow_ready")
        ada_flip = sem("ada_flip")
        mod_ready = sem("mod_ready")
        pro_mm = sem("pro_mm")
        pro_hi_ready = sem("pro_hi_ready")
        pro_lo_ready = sem("pro_lo_ready")
        pro_row = sem("pro_row")
        pro_flip = sem("pro_flip")
        s_split = sem("s_split")
        rows_t = sem("rows_t")
        cols_ready = sem("cols_ready")
        s_ready = sem("s_ready")
        xt_done = sem("xt_done")
        x_loaded = sem("x_loaded")
        gate_done = sem("gate_done")
        silu_done = sem("silu_done")
        up_done = sem("up_done")
        prod_done = sem("prod_done")
        ahi_done = sem("ahi_done")
        alo_done = sem("alo_done")
        down_done = sem("down_done")
        y_done = sem("y_done")
        y_out = sem("y_out")
        sq1_ready = sem("sq1_ready")
        sq1_used = sem("sq1_used")
        sq2_ready = sem("sq2_ready")
        sq2_used = sem("sq2_used")
        root_ready = sem("root_ready")
        inv_ready = sem("inv_ready")
        diag_ready = sem("diag_ready")
        spread = sem("spread")
        gain_ready = sem("gain_ready")
        upd_ready = sem("upd_ready")
        x_ready = sem("x_ready")
        xd_ready = sem("xd_ready")
        ht_ready = sem("ht_ready")
        hv_ready = sem("hv_ready")
        hh_ready = sem("hh_ready")
        hl_ready = sem("hl_ready")
        hd_ready = sem("hd_ready")
        mix_in = sem("mix_in")
        rq_ready = sem("rq_ready")
        mhalf_ready = sem("mhalf_ready")
        win_in = sem("win_in")
        toe_in = sem("toe_in")
        sink_in = sem("sink_in")
        toe_ready = sem("toe_ready")
        pe_step = sem("pe_step")
        act_step = sem("act_step")
        dve_step = sem("dve_step")
        ot_done = sem("ot_done")
        o_ready = sem("o_ready")
        out_done = sem("out_done")
        zero_ready = sem("zero_ready")

        MIX_IN = (7, 9)
        base, phase = 0, []
        for l in range(LAYERS):
            for kind in ("ffn0", "mix", "ffn1"):
                phase.append(base)
                base += 2 * GU_STEPS + DOWN_UNITS if kind != "mix" else MIX_IN[l] + 4
        phase.append(base)
        last_unit = base

        def kview(ap, lo_, n):
            return ap.rearrange("(k p) n -> p k n", p=P)[:, :, lo_:lo_ + n]

        w_ab, w_cd = ab_w_in[0], cd_w_in[0]
        mix_src = [
            [kview(w_ab, 0, 256), kview(w_ab, 256, 160), kview(mla_w_uq[0], 0, 768), kview(mla_w_ukv[0], 0, 1024),
             kview(w_ab, 928, 256), kview(w_ab, 416, 256), kview(w_ab, 672, 256)],
            [kview(w_cd, c0, 256) for c0 in (512, 0, 1792, 2048, 256, 1280, 1536, 768, 1024)],
        ]
        mix_out = [ab_w_out[0], cd_w_out[0]]

        def unit_width(n):
            for l in range(LAYERS):
                j = n - phase[3 * l + 1]
                if 0 <= j < MIX_IN[l]:
                    s = mix_src[l][j].shape
                    return s[1] * s[2]
            return UW

        ada_first, ada_norm = [], [None] * 6
        block = ADA_FFN
        for r in range(1, 6):
            ada_norm[r] = block
            block += 1
            if r % 3 == 1:
                ada_first.append(block)
                block += ADA_MIX[r // 3]
        assert ADA_PRO + block == ADA_ALL

        plans = []
        pe0 = act0 = dve0 = 0
        for l in range(LAYERS):
            toks, items = mixer_tokens(l, ada_first[l])
            pe = Steps([s for t in toks for s in pe_steps(t, l)], pe0)
            ac = Steps([s for t in toks for s in act_steps(t, l)], act0)
            dv_ = Steps([s for t in toks for s in dve_steps(t, l)], dve0)
            plans.append((toks, items, pe, ac, dv_))
            pe0, act0, dve0 = pe.end, ac.end, dv_.end

        unit_end = [
            {0: ("proj", "cq", 1), 1: ("proj", "kr", 0), 2: ("proj", "q", 7), 3: ("proj", "k", 7),
             4: ("proj", "bv", 0), 5: ("proj", "bq", 5), 6: ("proj", "bq", 7)},
            {0: ("proj", "cv", 0), 1: ("proj", "cq", 1), 2: ("proj", "dv", 1), 3: ("proj", "dv", 3),
             4: ("proj", "cq", 3), 5: ("proj", "dk", 1), 6: ("proj", "dk", 3), 7: ("proj", "dq", 5),
             8: ("proj", "dq", 7)},
        ]

        def work_order(l):
            o = []
            for t in plans[l][0]:
                if t[0] in ("proj", "turnv"):
                    o.append((t, "dve", t))
                elif t[0] == "norm" and t[1] == "bq":
                    o.append((("sum",) + t[1:], "dve", ("squares",) + t[1:]))
                elif t[0] in ("rank", "norm"):
                    o.append((("sum",) + t[1:], "act", ("root",) + t[1:]))
                elif t[0] == "rope":
                    o.append((t, "dve", ("sin",) + t[1:]))
            return o
        work = [work_order(l) for l in range(LAYERS)]

        B_WORK, B_ADA, B_S, B_PT, B_O = (0, 1), 2, (3, 4, 5), 6, 7
        B_ADA_NORM = 6

        def work_bank(l, name):
            i = [u[0] for u in work[l]].index(name)
            return ps[B_WORK[i % len(B_WORK)]]
        NW_POST = (NT, NT, NT, NT, LAT, LAT)
        NW_PRE = (NT, NT, NT, NT, NT, LAT)

        def bank_of(ch):
            return (ch + 4) % 8

        PRO_BANKS = (4, 6, 7, 3)
        SUM_W = 64
        SS1, SS2 = 4, 5

        ada_cols = ada_w.rearrange("l (k p) n -> l p k n", p=P)

        def ada_landed(k):
            return ada_in[k % 2], 16 * (k // 2 + 1)

        ADA_SPLIT = ADA_FFN * ADA_PCS + 1

        def ada_load(eng, k):
            if k >= 2:
                eng.wait_ge(ada_mm, k - 1)
            l, c0 = divmod((ADA_PRO + k // ADA_PCS) * ADA_W, 9 * D)
            kk = ADA_K * (k % ADA_PCS)
            eng.dma_start(ada_raw[:, k % 2, :, :], ada_cols[l][:, kk:kk + ADA_K, c0:c0 + ADA_W]).then_inc(ada_landed(k)[0], 16)

        def x_landed(b, ch):
            if ch < POOL_CH:
                return x_ready, POOL_CH * b + ch + 1
            return xd_ready, (KD - POOL_CH) * b + ch - POOL_CH + 1

        def h_landed(r, ch):
            if ch < POOL_CH:
                return hl_ready, POOL_CH * r + ch + 1
            return hd_ready, (KD - POOL_CH) * r + ch - POOL_CH + 1

        def ada_blocks(m):
            return m // ADA_CH - ADA_PRO + 1

        def wviews(n, k):
            w = wsp[n % 2]
            width = unit_width(n)
            return [w[:, h, 0:width].rearrange("p (k n) -> p k n", k=k) for h in range(2)]

        block = es.enter_context(nc.Block())

        @block.sync
        def _(sp):
            sp.dma_start(cst[:], consts[:, 0:K_KEEP]).then_inc(consts_in, 16)
            ab2 = ada_b.rearrange("l (r n) -> (l r) n", n=P)
            sp.dma_start(rows[:, 0, :], ab2[0:P, :]).then_inc(rows_in, 16)
            sp.dma_start(rows[0:16, 1, :], ab2[P:P + 16, :]).then_inc(rows_in, 16)
            sp.dma_start(rows[16:112, 1, :], norm_g.rearrange("l g (r n) -> (l g r) n", n=P)).then_inc(rows_in, 16)
            sp.dma_start(rows[112:120, 1, :], c.rearrange("b (r n) -> (b r) n", n=P)).then_inc(rows_in, 16)
            sp.dma_start(rows[120:128, 1, :], c_ctx.rearrange("(r n) -> r n", n=P)).then_inc(rows_in, 16)
            sp.dma_start(rows[0:2, 2, :], mla_q_norm.rearrange("b (r n) -> (b r) n", n=P)).then_inc(rows_in, 16)
            sp.dma_start(rows[2:3, 2, :], mla_kv_norm).then_inc(rows_in, 16)
            for r, g in ((3, gqa_q_norm), (4, gqa_k_norm)):
                for h in range(2):
                    sp.dma_start(rows[r:r + 1, 2, h * HD:(h + 1) * HD], g).then_inc(rows_in, 16)
            sp.dma_start(sinkc[:], swa_sink.broadcast_to([P, 8])).then_inc(sink_in, 16)
            xr = x[0].rearrange("(t p) n -> p t n", p=P)
            cr = ctx_x[0].rearrange("(t p) n -> p t n", p=P)
            yrow = Ysb[:, :, :].rearrange("p (t a) n -> p t (a n)", t=4)
            sp.dma_start(yrow[:, 0:2, :], xr).then_inc(x_in, 16)
            sp.dma_start(yrow[:, 2:4, :], cr).then_inc(x_in, 16)
            for i in range(4):
                w = ADA_PRO * ADA_W // 4
                sp.dma_start(ada_pro[:, :, i * w:(i + 1) * w], kview(ada_w[0], i * w, w)).then_inc(pro_in[i], 16)

            def free(n):
                sp.wait_ge(hi_ready, n - 1)
                sp.wait_ge(lo_ready, n - 1)

            def load(n, src, k):
                dst = raw[n % 2][:, 0:src.shape[1] * src.shape[2]].rearrange("p (k n) -> p k n", k=k)
                sp.dma_start(dst, src).then_inc(w_in[n % 2], 16)

            def ada_beside(r):
                for j in range(ADA_PCS):
                    if ada_norm[r] * ADA_PCS + j + 2 < (ADA_ALL - ADA_PRO) * ADA_PCS:
                        ada_load(sp, ada_norm[r] * ADA_PCS + j + 2)

            def ffn(n0, l, s):
                gate = ffn_w_gate[l, s].rearrange("(k p) n -> p k n", p=P)
                up = ffn_w_up[l, s].rearrange("(k p) n -> p k n", p=P)
                down = ffn_w_down[l, s].rearrange("(f p) n -> p f n", p=P)
                if n0 == 0:
                    ada_load(sp, 0)
                    load(0, gate[:, :, 0:UF], KD)
                    load(1, up[:, :, 0:UF], KD)
                    ada_load(sp, 1)
                    free(2)
                    load(2, gate[:, :, UF:2 * UF], KD)
                    free(3)
                    load(3, up[:, :, UF:2 * UF], KD)
                    with sp.Fori(0, ADA_FFN) as i:
                        for j in range(ADA_PCS):
                            sp.wait_ge(ada_mm, ADA_PCS * i + j + 1)
                            kk = ADA_K * ((2 + j) % ADA_PCS)
                            src = ada_cols[0][:, kk:kk + ADA_K, bass.ds((ADA_PRO + (2 + j) // ADA_PCS) * ADA_W + i * ADA_W, ADA_W)]
                            sp.dma_start(ada_raw[:, j % 2, :, :], src).then_inc(ada_in[j % 2], 16)
                            if j % 2 == 1:
                                part = j // 2
                                sp.wait_ge(hi_ready, 2 * i + part + 3)
                                sp.wait_ge(lo_ready, 2 * i + part + 3)
                                load(part, (gate, up)[part][:, :, bass.ds(i * UF + 2 * UF, UF)], KD)
                else:
                    for j, w in enumerate((gate, up)):
                        free(n0 + j)
                        load(n0 + j, w[:, :, 0:UF], KD)
                    ada_beside(3 * l + 2 * s)
                with sp.Fori(ADA_FFN + 2 if n0 == 0 else 1, GU_STEPS) as i:
                    for j, w in enumerate((gate, up)):
                        sp.wait_ge(hi_ready, n0 + 2 * i + j - 1)
                        sp.wait_ge(lo_ready, n0 + 2 * i + j - 1)
                        load(n0 + j, w[:, :, bass.ds(i * UF, UF)], KD)
                n1 = n0 + 2 * GU_STEPS
                with sp.Fori(0, DOWN_UNITS // 2) as i:
                    for j in range(2):
                        sp.wait_ge(hi_ready, n1 + 2 * i + j - 1)
                        sp.wait_ge(lo_ready, n1 + 2 * i + j - 1)
                        load(n1 + j, down[:, bass.ds(4 * i + 2 * j, 2), :], 2)
                free(n1 + DOWN_UNITS - 1)
                load(n1 + DOWN_UNITS - 1, down[:, 2 * (DOWN_UNITS - 1):, :], 2)

            for l in range(LAYERS):
                ffn(phase[3 * l], l, 0)
                mc = (mc0, mc1)[l]
                n0 = phase[3 * l + 1]

                def mixer_unit(j):
                    free(n0 + j)
                    if j < MIX_IN[l]:
                        load(n0 + j, mix_src[l][j], mix_src[l][j].shape[1])
                    else:
                        f = 2 * (j - MIX_IN[l])
                        load(n0 + j, mix_out[l].rearrange("(f p) n -> p f n", p=P)[:, f:f + 2, :], 2)

                mixer_unit(0)
                mixer_unit(1)
                ada_beside(3 * l + 1)
                sp.wait_ge(y_done, 8 * (3 * l + 1))
                sp.dma_start(mc[:], consts[:, K_KEEP:K_KEEP + mc.shape[1]]).then_inc(mix_in, 16)
                mixer_unit(2)
                mixer_unit(3)
                if l == 1:
                    sp.wait_ge(win_in, 16 * 8)
                    for half in range(2):
                        for h in range(8):
                            src = bass.AP(tensor=rpb_win.tensor,
                                          offset=rpb_win.offset + h * 7 * GRID * 127 + (1 - half) * GRID * 127 + 63,
                                          ap=[[126, GRID], [GRID * 127, 6], [1, GRID]])
                            sp.dma_start(toe[half * GRID:(half + 1) * GRID, h, :, :], src).then_inc(toe_in, 16)
                waiting, pieces = [], 0
                for t in plans[l][0]:
                    if t[0] == "split":
                        waiting.append((t[1] + 2, pieces + 2))
                    elif t[0] == "ada":
                        pieces += 1
                        if t[1] + 2 < (ADA_ALL - ADA_PRO) * ADA_PCS:
                            ada_load(sp, t[1] + 2)
                    while waiting and (waiting[0][1] <= pieces or len(waiting) > 1):
                        mixer_unit(waiting.pop(0)[0])
                for unit, _ in waiting:
                    mixer_unit(unit)
                ffn(phase[3 * l + 2], l, 1)
            for t in range(2):
                sp.wait_ge(o_ready, 2 * (t + 1))
                sp.dma_start(out[0, t * P:(t + 1) * P, :], outs[:, t, :]).then_inc(out_done, 16)
            sp.wait_ge(out_done, 32)

        @block.gpsimd
        def _(pool):
            def residual(b):
                w = NW_POST[b]
                for ch in range(POOL_CH):
                    pool.wait_ge(upd_ready, KD * b + ch + 1)
                    pool.tensor_tensor(X[:, ch, 0:w], X[:, ch, 0:w], Ysb[:, ch, 0:w], ALU.add).then_inc(x_ready, 1)

            def low(r):
                w = NW_PRE[r]
                for ch in range(POOL_CH):
                    pool.wait_ge(hh_ready, KD * r + ch + 1)
                    pool.tensor_tensor(H[:, ch, 1, 0:w], h_whole[:, ch, 1, 0:w], H[:, ch, 0, 0:w].bitcast(F32), ALU.subtract).then_inc(hl_ready, 1)

            def bias_masks():
                pool.wait_ge(toe_in, 16 * 16)
                pool.wait_ge(mix_in, 32)
                mask = mc1[:, M_NA:M_NA + GRID].rearrange("p (a n) -> p a n", a=1).broadcast_to([P, 6, GRID])
                for h in range(8):
                    pool.tensor_tensor(toe[:, h, :, :], toe[:, h, :, :], mask, ALU.add).then_inc(toe_ready, 1)

            def mixer(l, b):
                toks, _, pe, ac, dv_ = plans[l]
                n0 = phase[b]
                if l == 0:
                    pool.memset(mhalf[:], -0.5).then_inc(mhalf_ready, 1)
                for t in toks:
                    if t[0] == "split":
                        n, w = n0 + t[1], unit_width(n0 + t[1])
                        pool.wait_ge(pe_step, pe.at(*unit_end[l][t[1] - 2]))
                        pool.wait_ge(w_in[n % 2], 16 * (n // 2 + 1))
                        pool.tensor_copy(wsp[n % 2][:, 0, 0:w], raw[n % 2][:, 0:w]).then_inc(hi_ready, 1)
                        pool.wait_ge(hi_ready, n + 1)
                        pool.tensor_tensor(wsp[n % 2][:, 1, 0:w], raw[n % 2][:, 0:w], wsp[n % 2][:, 0, 0:w].bitcast(F32),
                                           ALU.subtract).then_inc(lo_ready, 1)
                        if l == 1 and t[1] == 3:
                            bias_masks()
                    elif t[:2] == ("norm", "bq"):
                        p = t[2]
                        pool.wait_ge(dve_step, dv_.at("squares", "bq", p))
                        if p == 4:
                            pool.wait_ge(mhalf_ready, 1)
                        if p >= 6:
                            pool.wait_ge(act_step, ac.at("exp", 8 * (p - 1) - 1))
                        pool.tensor_tensor(rq[:, p % 2, :], ssq[:, p % 2, :], mhalf[:], ALU.pow).then_inc(rq_ready, 1)

            low(0)
            for h in range(8):
                src = bass.AP(tensor=na_rpb.tensor, offset=na_rpb.offset + h * 465 + 4 * 31 + 15 - 63,
                              ap=[[31, 7], [0, GRID], [1, 127]])
                pool.dma_start(rpb_win[h], src).then_inc(win_in, 16)
            residual(0)
            low(1)
            mixer(0, 1)
            residual(1)
            low(2)
            residual(2)
            low(3)
            residual(3)
            low(4)
            mixer(1, 4)
            residual(4)
            low(5)
            residual(5)

        @block.tensor
        def _(pe):
            mm = nc.tensor.matmul

            def mm3(o, w, v, start, stop):
                mm(o, w[0], v[0], start=start, stop=False)
                mm(o, w[0], v[1], start=False, stop=False)
                return mm(o, w[1], v[0], start=False, stop=stop)

            def hl(t, k, c0, c1):
                return t[:, k, 0, c0:c1], t[:, k, 1, c0:c1]

            def ada_piece(slot, j, bank, split):
                for kk in range(ADA_K):
                    k = ADA_K * j + kk
                    start, stop = k == 0, k == KD - 1
                    o = ps[bank][0:4, :]
                    if split:
                        mm(o, sS[:, k, :], ada_hi[:, kk, :], start=start, stop=False)
                        last = mm(o, sS[:, k, :], ada_lo[:, slot, kk, :], start=False, stop=stop)
                    else:
                        last = mm(o, sT[:, k, :], ada_raw[:, slot, kk, :], start=start, stop=stop)
                last.then_inc(ada_mm, 1)

            def ada_fold(bank, ch, row):
                return mm(ps[bank][:, 2 * ch:2 * ch + 2], row, fold[:], start=True, stop=True)

            def ada_turn(bank):
                for ch in range(ADA_CH):
                    last = ada_fold(bank, ch, arow[:, ch * P:(ch + 1) * P])
                last.then_inc(ada_flip, 1)

            def sum_sq(ready, used, bank, b, ch, w):
                pe.wait_ge(ready, KD * b + ch + 1)
                for t in range(w // P):
                    last = mm(ps[bank][:, t * SUM_W:(t + 1) * SUM_W], T[ch % 2][:, t * P:(t + 1) * P], ones[:, 0:SUM_W],
                              start=ch == 0 and t == 0, stop=ch == KD - 1, skip_group_check=True)
                last.then_inc(used, 1)

            def spread_inv(n, bank, w):
                pe.wait_ge(diag_ready, n)
                mm(ps[bank][:, 0:w], ones, T[2][:, 0:w], start=True, stop=True).then_inc(spread, 1)

            def ada_beside(r, j):
                k = ada_norm[r] * ADA_PCS + j
                if k < ADA_SPLIT:
                    pe.wait_ge(ada_lo_ready, k + 1)
                else:
                    pe.wait_ge(*ada_landed(k))
                if j == 0:
                    pe.wait_ge(y_out, KD * r)
                ada_piece(k % 2, j, B_ADA_NORM, k < ADA_SPLIT)

            def pre_sums(r, w):
                for ch in range(KD):
                    if r and ch in (0, 2):
                        for j in {0: (0, 1), 2: (2,)}[ch]:
                            ada_beside(r, j)
                    sum_sq(sq2_ready, sq2_used, SS2, r, ch, w)
                if r:
                    ada_beside(r, 3)
                if r:
                    spread_inv(2 * r + 1, SS2, w)
                    pe.wait_ge(arow_ready, ada_norm[r] + 1)
                    ada_turn(B_ADA_NORM)

            def ffn(q, n0, r, l, s):
                w = NW_PRE[r]

                def gate_up(lo_, hi_, with_ada):
                    with pe.Fori(lo_, hi_) as i:
                        for part, (done, free) in enumerate(((gate_done, silu_done), (up_done, prod_done))):
                            pe.wait_ge(hi_ready, n0 + 2 * i + part + 1)
                            pe.wait_ge(lo_ready, n0 + 2 * i + part + 1)
                            W = wviews(n0 + part, KD)
                            for j in range(2):
                                pe.wait_ge(free, q * NF + 2 * i + j + 1)
                                o = ps[2 * part + j][:, 0:w]
                                for k in range(KD):
                                    if part == 0 and j == 0:
                                        pe.wait_ge(*h_landed(r, k))
                                    lw = [W[h][:, k, j * P:(j + 1) * P] for h in range(2)]
                                    pc = 2 * part + j
                                    if with_ada and k == 4:
                                        pe.wait_ge(ada_lo_ready, ADA_PCS * i + pc + 1)
                                        if pc == 0:
                                            pe.wait_ge(mod_ready, i + 1)
                                        ada_piece(j, pc, 4, True)
                                    if with_ada and k == KD - 1 and pc == 3:
                                        pe.wait_ge(arow_ready, i + 1)
                                    last = mm3(o, lw, hl(H, k, 0, w), k == 0, k == KD - 1)
                                last.then_inc(done, 1)
                            if with_ada and part == 1:
                                ada_turn(4)

                if q == 0:
                    gate_up(0, ADA_FFN, True)
                gate_up(ADA_FFN if q == 0 else 0, GU_STEPS, False)
                down(n0 + 2 * GU_STEPS, DOWN_UNITS, r, w, q)

            def down(n1, units, b, w, q):
                def unit(n, f0, start, stop, pair=None):
                    pe.wait_ge(hi_ready, n + 1)
                    pe.wait_ge(lo_ready, n + 1)
                    W = wviews(n if pair is None else pair, 2)
                    for ch in range(KD):
                        for f in range(2):
                            lw = [W[h][:, f, ch * P:(ch + 1) * P] for h in range(2)]
                            if isinstance(f0, int):
                                v = hl(A, f0 + f, 0, w)
                            else:
                                v = [A[:, bass.ds(f0 + f, 1), h, 0:w].rearrange("p a n -> p (a n)") for h in range(2)]
                            last = mm3(ps[bank_of(ch)][:, 0:w], lw, v, start and f == 0, stop and f == 1)
                        if stop:
                            last.then_inc(y_done, 1)
                            if ch >= 2:
                                sum_sq(sq1_ready, sq1_used, SS1, b, ch - 2, w)
                    if not stop:
                        last.then_inc(down_done, 1)

                if q is not None:
                    pe.wait_ge(mod_ready, ada_norm[b] + 2 if b else ADA_FFN + 1)
                    pe.wait_ge(silu_done, (q + 1) * NF + 2)
                    pe.wait_ge(alo_done, (q + 1) * NF + 2)
                unit(n1, 0, True, False)
                if units == DOWN_UNITS:
                    unit(n1 + 1, 2, False, False)
                    with pe.Fori(1, 4) as i:
                        for j in range(2):
                            unit(n1 + 2 * i + j, 4 * i + 2 * j, False, False, pair=n1 + j)
                    for u in (8, 9):
                        unit(n1 + u, 2 * u, False, False)
                else:
                    for u in range(1, units - 1):
                        unit(n1 + u, 2 * u, False, False)
                unit(n1 + units - 1, 2 * (units - 1), False, True)
                for ch in (6, 7):
                    sum_sq(sq1_ready, sq1_used, SS1, b, ch, w)
                spread_inv(2 * b + 2, SS1, w)

            def mixer(l, b):
                toks, items, st, ac, dv_ = plans[l]
                n0 = phase[b]
                mc = (mc0, mc1)[l]
                qh, kh, pp, pt = (qh0, kh0, probs[0], pt0) if l == 0 else (qh1, None, probs[1], pt1)
                kd_ = (kdup0, kdup1)[l]
                tiles = 4 if l == 0 else 2
                pe.wait_ge(mix_in, 16 * (l + 1))

                def use(j):
                    pe.wait_ge(hi_ready, n0 + j + 1)
                    pe.wait_ge(lo_ready, n0 + j + 1)
                    return wviews(n0 + j, mix_src[l][j].shape[1])

                def features(o, W, c0, m, w, h_waits=False):
                    for k in range(KD):
                        if h_waits:
                            pe.wait_ge(*h_landed(b, k))
                        last = mm3(o, [W[h][:, k, c0:c0 + m] for h in range(2)], hl(H, k, 0, w), k == 0, k == KD - 1)
                    return last

                def by_token(o, W, c0, n, t):
                    for k in range(KD):
                        last = mm3(o, [x_ for x_ in hl(H, k, t * P, (t + 1) * P)], [W[h][:, k, c0:c0 + n] for h in range(2)],
                                   k == 0, k == KD - 1)
                    return last

                def work_free(name):
                    i = [u[0] for u in work[l]].index(name) - len(B_WORK)
                    if i >= 0:
                        _, eng, reader = work[l][i]
                        pe.wait_ge(act_step if eng == "act" else dve_step, (ac if eng == "act" else dv_).at(*reader))

                first_proj = work[l][0][0]
                for t in toks:
                    k = t[0]
                    if k == "proj":
                        work_free(t)
                        h_waits = t is first_proj
                        o = work_bank(l, t)
                        what, j = t[1:]
                        if (l, what) == (0, "cq"):
                            last = features(o[:, 0:NT], use(0), j * P, P, NT, h_waits)
                        elif what == "ckv":
                            last = features(o[:, 0:NT], use(1), 0, P, NT)
                        elif what == "kr":
                            last = features(o[0:32, 0:NT], use(1), P, 32, NT)
                        elif what == "va":
                            W = use(3)
                            pe.wait_ge(dve_step, dv_.at("lo", "ckv", 0))
                            wv = [W[h][:, 0, :].rearrange("p (h e) -> p h e", e=P)[:, :, HD:P] for h in range(2)]
                            last = mm3(o[:, 0:512].rearrange("p (h e) -> p h e", e=HD),
                                       [ckvn[:, h, j * P:(j + 1) * P] for h in range(2)], wv, True, True)
                        elif what == "q":
                            W = use(2)
                            pe.wait_ge(dve_step, dv_.at("lo", "cq", 1))
                            for kk in range(2):
                                last = mm3(o[0:QK, 0:NT], [W[h][:, kk, j * QK:(j + 1) * QK] for h in range(2)],
                                           [cqn[:, kk, h, :] for h in range(2)], kk == 0, kk == 1)
                        elif what == "k":
                            W = use(3)
                            pe.wait_ge(dve_step, dv_.at("lo", "ckv", 0))
                            last = mm3(o[0:HD, 0:NT], [W[h][:, 0, j * P:j * P + HD] for h in range(2)],
                                       [ckvn[:, h, :] for h in range(2)], True, True)
                        elif what in ("bk", "ck"):
                            last = features(o[:, 0:NT], use(4 if l == 0 else 0), 0, P, NT, h_waits)
                        elif what in ("bv", "cv"):
                            last = features(o[:, 0:NT], use(4 if l == 0 else 0), P, P, NT)
                        elif what == "bq":
                            last = features(o[:, 0:NT], use(5 + (j - 4) // 2), (j % 2) * P, P, NT)
                        elif what == "dv":
                            W = use(2 + j // 2)
                            for tt in range(2):
                                last = by_token(o[:, tt * 256:(tt + 1) * 256], W, 0, 256, 2 * (j % 2) + tt)
                        elif what == "dk":
                            last = features(o[:, 0:NT], use(5 + j // 2), (j % 2) * P, P, NT)
                        elif what == "cq":
                            last = features(o[:, 0:LAT], use(1 + 3 * (j // 2)), (j % 2) * P, P, LAT)
                        elif what == "dq":
                            last = features(o[:, 0:LAT], use(7 + (j - 4) // 2), (j % 2) * P, P, LAT)
                        st.did(pe_step, last, *t)
                    elif k == "turnv":
                        work_free(t)
                        pe.wait_ge(dve_step, dv_.at("proj", t[1], 0))
                        for tt in range(4):
                            c_ = slice(tt * P, (tt + 1) * P)
                            last = nc.tensor.transpose(work_bank(l, t)[:, c_], vbuf[t[1]][:, c_], ident)
                        st.did(pe_step, last, *t)
                    elif k in ("rank", "norm"):
                        name = ("sum",) + t[1:]
                        work_free(name)
                        n = 2 if t[1] == "cq" else 1
                        if t[1] == "bq":
                            pe.wait_ge(act_step, ac.at("square", t[1], t[2], 0))
                            for tt in range(4):
                                last = mm(work_bank(l, name)[:, 2 * tt:2 * tt + 2], T[0][:, tt * P:(tt + 1) * P],
                                          mc[:, M_BLK:M_BLK + P:HD], start=True, stop=True)
                            n = 0
                        for i in range(n):
                            pe.wait_ge(act_step, ac.at("square", t[1], t[2], i))
                            lw = ones if k == "rank" else mc[:, M_BLK:M_BLK + P]
                            last = mm(work_bank(l, name)[:, 0:NT], lw, T[i][:, 0:NT], start=i == 0, stop=i == n - 1)
                        st.did(pe_step, last, *name)
                    elif k == "ada":
                        pe.wait_ge(*ada_landed(t[1]))
                        if t[1] % ADA_PCS == 0:
                            pe.wait_ge(mod_ready, t[1] // ADA_PCS + 1)
                            if t[1] // ADA_PCS == ada_first[l]:
                                pe.wait_ge(y_out, KD * b)
                        ada_piece(t[1] % 2, t[1] % ADA_PCS, B_ADA, False)
                    elif k == "flip":
                        pe.wait_ge(arow_ready, t[1] + 1)
                        ada_turn(B_ADA)
                    elif k == "rope":
                        work_free(t)
                        what, j = t[1:]
                        ax = work_bank(l, t)
                        if what == "q":
                            pe.wait_ge(dve_step, dv_.at("proj", "q", j))
                            last = mm(ax[0:QK, 0:LAT], mc[0:QK, M_P96:M_P96 + QK], qh[j % 4][0:QK, 0:LAT], start=True, stop=True)
                        elif what == "kr":
                            pe.wait_ge(dve_step, dv_.at("proj", "kr", 0))
                            last = mm(ax[0:QK, 0:LAT], mc[0:QK, M_P96:M_P96 + QK], T[3][0:QK, 0:LAT], start=True, stop=True)
                        else:
                            src = kbuf.get(what, qh[j % 2])
                            pe.wait_ge(dve_step, dv_.at("normed", what, j) if what == "bk" else dv_.at("proj", what, j))
                            last = mm(ax[:, 0:LAT], mc[:, M_P64:M_P64 + P], src[:, 0:LAT], start=True, stop=True)
                        st.did(pe_step, last, *t)
                    elif k == "score":
                        i = t[1]
                        p, e, tt = items[i]
                        if i >= DEEP:
                            pe.wait_ge(act_step, ac.at("exp", i - DEEP))
                        if l == 0 and p < 4:
                            h = 2 * p + e
                            pe.wait_ge(dve_step, max(dv_.at("rope", "q", h), dv_.at("proj", "k", h), dv_.at("dup", "kr", 0)))
                            lhs, rhs = qh[h % 4][0:QK, :], kh[h % 4][0:QK, :]
                        else:
                            g = slice(e * HD, (e + 1) * HD)
                            if l == 0 or p < 4:
                                need = ("rope", "bq" if l == 0 else "cq", p)
                                rhs = kd_[(p % 4) // 2][g, :]
                            else:
                                need = ("proj", "dq", p)
                                rhs = dk[g, p - 4, :]
                            pe.wait_ge(dve_step, dv_.at(*need))
                            lhs = qh[p % 2][g, :]
                        k0_ = 0 if tt < 2 else LAT
                        last = mm(ps[B_S[i % DEEP]][:, k0_:NT], lhs[:, tt * P:(tt + 1) * P], rhs[:, k0_:NT], start=True, stop=True)
                        st.did(pe_step, last, *t)
                    elif k == "turn":
                        i = t[1]
                        tt = items[i][2]
                        pe.wait_ge(dve_step, dv_.at("prob", i))
                        if i == 0:
                            pe.wait_ge(mod_ready, ada_norm[b] + 2)
                        if i >= 1:
                            pe.wait_ge(act_step, ac.at("turn", i - 1))
                        for kt in range(0 if tt < 2 else 2, 4):
                            last = nc.tensor.transpose(ps[B_PT][:, kt * P:(kt + 1) * P], pp[i % DEEP][:, kt * P:(kt + 1) * P], ident)
                        st.did(pe_step, last, *t)
                    elif k == "value":
                        i = t[1]
                        p, e, tt = items[i]
                        pe.wait_ge(act_step, ac.at("turn", i))
                        if e == 0 and tt == 0 and p:
                            pe.wait_ge(dve_step, dv_.at("out", p - 1))
                        if l == 0:
                            v, c0 = (va, (2 * p + e) * HD) if p < 4 else (vb, ((p - 4) // 2) * HD)
                        else:
                            v, c0 = (cv, (p // 2) * HD) if p < 4 else (dv, (2 * (p - 4) + e) * HD)
                        first = 0 if tt < 2 else 2
                        for kt in range(first, 4):
                            last = mm(ps[B_O][e * HD:(e + 1) * HD, tt * P:(tt + 1) * P], v[:, kt, c0:c0 + HD],
                                      pt[i % 2][:, kt, :], start=kt == first, stop=kt == 3)
                        st.did(pe_step, last, *t)
                pe.wait_ge(dve_step, dv_.at("out", 7))
                down(n0 + MIX_IN[l], 4, b, NW_POST[b], None)

            pe.wait_ge(consts_in, 16)
            pe.wait_ge(rows_in, 16 * 11)
            for i, n in enumerate((P, P, 5)):
                nc.tensor.transpose(ps[i][:, 0:n], rows[0:n, i, :], ident[0:n, 0:n]).then_inc(rows_t, 1)
            pe.wait_ge(x_in, 32)
            xrow = Ysb[:, :, :].rearrange("p (t a) n -> p t (a n)", t=4)
            for i, ch in enumerate((3, 4, 5, 6, 7, 0, 1, 2)):
                if ch < 3:
                    pe.wait_ge(cols_ready, 3)
                for t in range(4):
                    last = nc.tensor.transpose(ps[ch][:, t * P:(t + 1) * P], xrow[:, t, ch * P:(ch + 1) * P], ident)
                last.then_inc(xt_done, 1)
            pe.wait_ge(x_loaded, 8)
            pe.wait_ge(s_ready, 2)

            def pro_block(i):
                pe.wait_ge(pro_in[i], 16)
                if i >= 2:
                    pe.wait_ge(pro_lo_ready, i - 1)
                o = ps[PRO_BANKS[i]][0:4, :]
                for kk in range(KD):
                    c_ = slice(i * ADA_W, (i + 1) * ADA_W)
                    start, stop = kk == 0, kk == KD - 1
                    if i >= 2:
                        mm(o, sS[:, kk, :], pro_his[i - 2][:, kk, :], start=start, stop=False)
                        last = mm(o, sS[:, kk, :], pro_lo[:, kk, c_], start=False, stop=stop)
                    else:
                        last = mm(o, sT[:, kk, :], ada_pro[:, kk, c_], start=start, stop=stop)
                last.then_inc(pro_mm, 1)

            def pro_turn(i):
                pe.wait_ge(pro_row, i + 1)
                for j in range(ADA_CH):
                    last = ada_fold(PRO_BANKS[0], ADA_CH * i + j, Ysb[0:4, i, j * P:(j + 1) * P])
                if i == ADA_PRO - 1:
                    last.then_inc(pro_flip, 1)

            pro_block(0)
            pre_sums(0, NT)
            pro_block(1)
            spread_inv(1, SS2, NT)
            pro_turn(0)
            pro_block(2)
            pro_turn(1)
            pro_block(3)
            pro_turn(2)
            pro_turn(3)

            for l in range(LAYERS):
                ffn(2 * l, phase[3 * l], 3 * l, l, 0)
                pre_sums(3 * l + 1, NW_PRE[3 * l + 1])
                mixer(l, 3 * l + 1)
                pre_sums(3 * l + 2, NW_PRE[3 * l + 2])
                ffn(2 * l + 1, phase[3 * l + 2], 3 * l + 2, l, 1)
                if l + 1 < LAYERS:
                    pre_sums(3 * l + 3, NW_PRE[3 * l + 3])
            for ch in range(KD):
                pe.wait_ge(*x_landed(5, ch))
            for t in range(2):
                for half in range(2):
                    for j in range(4):
                        ch = 4 * half + j
                        last = nc.tensor.transpose(ps[2 * t + half][:, j * P:(j + 1) * P], X[:, ch, t * P:(t + 1) * P], ident)
                    last.then_inc(ot_done, 1)

        @block.scalar
        def _(act):
            A_ = nc.scalar.activation

            def copy(o, i):
                return A_(o, i, ACT.Copy)

            def split_hi(n, used, value, reg=None):
                if used is not None:
                    act.wait_ge(used, value)
                w = unit_width(n if reg is None else n + reg[1])
                act.wait_ge(w_in[n % 2], 16 * (n // 2 + 1) if reg is None else 16 * (n // 2 + reg[0] + 1))
                copy(wsp[n % 2][:, 0, 0:w], raw[n % 2][:, 0:w]).then_inc(hi_ready, 1)

            def post(b):
                w = NW_POST[b]
                A_(spare[:], epsc[:], ACT.Sqrt)
                for ch in range(KD):
                    act.wait_ge(y_out, KD * b + ch + 1)
                    if ch >= 2:
                        act.wait_ge(sq1_used, KD * b + ch - 1)
                    A_(T[ch % 2][:, 0:w], Ysb[:, ch, 0:w], ACT.Square).then_inc(sq1_ready, 1)
                act.wait_ge(sq1_used, KD * (b + 1))
                A_(rcol[:, 0:w // P], ps[SS1][:, 0:SUM_W * w // P:SUM_W], ACT.Sqrt, bias=epsc[:, 0:1], scale=1.0 / D).then_inc(root_ready, 1)

            def pre(r):
                w = NW_PRE[r]
                for ch in range(KD):
                    if r == 0:
                        act.wait_ge(x_loaded, 8)
                    else:
                        act.wait_ge(*x_landed(r - 1, ch))
                    if ch >= 2:
                        act.wait_ge(sq2_used, KD * r + ch - 1)
                    A_(T[ch % 2][:, 0:w], X[:, ch, 0:w], ACT.Square).then_inc(sq2_ready, 1)
                act.wait_ge(sq2_used, KD * (r + 1))
                A_(rcol[:, 0:w // P], ps[SS2][:, 0:SUM_W * w // P:SUM_W], ACT.Sqrt, bias=epsc[:, 0:1], scale=1.0 / D).then_inc(root_ready, 1)
                if r == 0:
                    def row(i):
                        act.wait_ge(pro_mm, i + 1)
                        copy(Ysb[0:4, i, :], ps[PRO_BANKS[i]][0:4, :]).then_inc(pro_row, 1)

                    row(0)
                    for i in (2, 3):
                        act.wait_ge(pro_in[i], 16)
                        copy(pro_his[i - 2][:, :, :], ada_pro[:, :, i * ADA_W:(i + 1) * ADA_W]).then_inc(pro_hi_ready, 1)
                    row(1)
                    ada_high(0, 16, None)
                    split_hi(0, None, 0)
                    row(2)
                    row(3)
                m0_ = (r // 3) * 72 + (r % 3) * 24
                if r:
                    ada_row((ada_norm[r] + 1) * ADA_PCS, B_ADA_NORM)
                act.wait_ge(mod_ready, ada_blocks(m0_ + 16))
                for ch in range(KD):
                    act.wait_ge(ht_ready, KD * r + ch + 1)
                    for s in range(w // LAT):
                        c_ = slice(s * LAT, (s + 1) * LAT)
                        last = A_(h_whole[:, ch, 1, c_], h_whole[:, ch, 1, c_], ACT.Identity,
                                  bias=mod[:, m0_ + ch, s:s + 1], scale=scol[:, ch, s:s + 1])
                    last.then_inc(hv_ready, 1)

            def ada_row(piece_count, bank):
                act.wait_ge(ada_mm, piece_count)
                copy(arow[:], ps[bank][0:4, :]).then_inc(arow_ready, 1)

            def ada_high(slot, landed, used, flipped=None):
                act.wait_ge(ada_in[slot], landed)
                if used is not None:
                    act.wait_ge(ada_mm, used)
                if flipped is not None:
                    act.wait_ge(ada_flip, flipped)
                copy(ada_hi[:], ada_raw[:, slot, :, :]).then_inc(ada_hi_ready, 1)

            def gate_up(q, n0, w):
                def steps(lo_, hi_, with_ada):
                    with act.Fori(lo_, hi_) as i:
                        for j in range(2):
                            if with_ada:
                                ada_high(1 - j, 32 * i + 16 * (j + 1), ADA_PCS * i + j + 1)
                            act.wait_ge(gate_done, q * NF + 2 * i + j + 1)
                            act.wait_ge(alo_done, q * NF + 2 * i + j + 1)
                            A_(T[j][:, 0:w], ps[j][:, 0:w], ACT.Silu).then_inc(silu_done, 1)
                        split_hi(n0 + 2, gate_done, q * NF + 2 * i + 2, reg=(i, 0))
                        if with_ada:
                            ada_high(1, 32 * i + 32, ADA_PCS * i + 3)
                        for j in range(2):
                            act.wait_ge(prod_done, q * NF + 2 * i + j + 3)
                            copy(A[:, bass.ds(2 * i + j, 1), 0, 0:w].rearrange("p a n -> p (a n)"), T[j][:, 0:w]).then_inc(ahi_done, 1)
                            if with_ada and j == 0:
                                ada_row(ADA_PCS * i + ADA_PCS, 4)
                                ada_high(0, 32 * i + 48, ADA_PCS * i + 4, i + 1)
                        split_hi(n0 + 3, up_done, q * NF + 2 * i + 2, reg=(i, 0))

                if q == 0:
                    steps(0, ADA_FFN, True)
                steps(ADA_FFN if q == 0 else 0, GU_STEPS, False)

            def down_splits(n1, units, d0, b):
                if units == DOWN_UNITS:
                    for u in range(2):
                        split_hi(n1 + u + 2, down_done, d0 + u + 1)
                    with act.Fori(1, 4) as i:
                        for j in range(2):
                            split_hi(n1 + 2 + j, down_done, d0 + 2 * i + j + 1, reg=(i, 0))
                    rest = (8, 9)
                else:
                    rest = range(units - 1)
                    act.wait_ge(lo_ready, n1 + 2)
                for u in rest:
                    if n1 + u + 2 < last_unit:
                        split_hi(n1 + u + 2, down_done, d0 + u + 1)

            def last_split(n1, units, b):
                if n1 + units + 1 < last_unit:
                    split_hi(n1 + units + 1, y_done, KD * (b + 1))

            def mixer(l, b):
                toks, items, pe, st, dv_ = plans[l]
                n0 = phase[b]
                pp, pt = probs[l], (pt0, pt1)[l]
                for t in toks:
                    k = t[0]
                    if k == "proj" and t[1] == "bq":
                        act.wait_ge(pe_step, pe.at("proj", "bq", t[2]))
                        before = [u for u in toks[:toks.index(t)] if u[0] == "rope"][-1]
                        act.wait_ge(dve_step, dv_.at(*before))
                        st.did(act_step, A_(T[0][:], work_bank(l, ("proj", "bq", t[2]))[:], ACT.Square), "square", "bq", t[2], 0)
                    elif k in ("rank", "norm") and t[1] != "bq":
                        n = 2 if t[1] == "cq" else 1
                        src = {"cq": [qh0[0], qh0[1]], "ckv": [qh0[2]], "bk": [kbuf["bk"]]}.get(t[1]) or [qh0[t[2] % 2]]
                        for i in range(n):
                            act.wait_ge(dve_step, dv_.at("proj", t[1], i if t[1] == "cq" else t[2]))
                            name = ("square", t[1], t[2], i)
                            st.did(act_step, A_(T[i][:], src[i][:], ACT.Square), *name)
                        act.wait_ge(pe_step, pe.at("sum", t[1], t[2]))
                        d_ = {"cq": 2 * P, "ckv": P}.get(t[1], HD)
                        st.did(act_step, A_(Rm[:], work_bank(l, ("sum", t[1], t[2]))[:, 0:NT], ACT.Sqrt, bias=epsc[:, 0:1], scale=1.0 / d_), "root", *t[1:])
                        if k == "rank":
                            for i in range(n):
                                act.wait_ge(dve_step, dv_.at("scaled", t[1], i))
                                dst = cqn[:, i, 0, :] if t[1] == "cq" else ckvn[:, 0, :]
                                st.did(act_step, copy(dst, src[i][:]), "hi", t[1], i)
                    elif k == "score":
                        i = t[1]
                        p, e, tt = items[i]
                        k0_ = 0 if tt < 2 else LAT
                        sink = l == 1 and i < 16
                        scaled = l == 0 and i >= 32
                        act.wait_ge(dve_step, dv_.at("sinkmax" if sink else "scaledmax" if scaled else "max", i))
                        if i >= DEEP:
                            act.wait_ge(pe_step, pe.at("turn", i - DEEP))
                        st.did(act_step, A_(pp[i % DEEP][:, k0_:NT], ps[B_S[i % DEEP]][:, k0_:NT], ACT.Exp, bias=nmax[:, i % DEEP:i % DEEP + 1],
                                            scale=rq[:, p % 2, 2 * tt + e:2 * tt + e + 1] if scaled else 1.0,
                                            accum_out=psum_[:, i % DEEP:i % DEEP + 1]), "exp", i)
                        if sink:
                            st.did(act_step, A_(sexp[:, i % DEEP:i % DEEP + 1], sinkc[:, 2 * p + e:2 * p + e + 1], ACT.Exp,
                                                bias=nmax[:, i % DEEP:i % DEEP + 1]), "sinkexp", i)
                    elif k == "ada":
                        if (t[1] + 1) % ADA_PCS == 0:
                            ada_row(t[1] + 1, B_ADA)
                    elif k == "turn":
                        i = t[1]
                        a = 0 if items[i][2] < 2 else 2
                        act.wait_ge(pe_step, pe.at("turn", i))
                        if i >= 2:
                            act.wait_ge(pe_step, pe.at("value", i - 2))
                        st.did(act_step, copy(pt[i % 2][:, a:4, :].rearrange("p a n -> p (a n)"), ps[B_PT][:, a * P:NT]), "turn", i)
                    elif k == "out":
                        p = t[1]
                        w = NW_POST[b]
                        act.wait_ge(pe_step, pe.at("value", (p + 1) * (8 if l == 0 else 4) - 1))
                        st.did(act_step, copy(A[:, p, 0, 0:w], ps[B_O][:, 0:w]), "out", p)

            act.sem_inc(silu_done, 2)
            act.wait_ge(cols_ready, 3)
            for s, c0 in ((0, C_C), (1, C_CC)):
                A_(sT[:, :, s], cols[:, c0:c0 + KD], ACT.Silu).then_inc(s_ready, 1)
            act.wait_ge(s_ready, 2)
            copy(sS[:, :, 0:2], sT[:, :, 0:2]).then_inc(s_split, 1)
            act.wait_ge(zero_ready, 1)
            A_(spare[:], epsc[:], ACT.Sqrt)
            pre(0)
            split_hi(1, None, 0)
            for l in range(LAYERS):
                d0 = l * (2 * (DOWN_UNITS - 1) + 3)
                gate_up(2 * l, phase[3 * l], NW_PRE[3 * l])
                down_splits(phase[3 * l] + 2 * GU_STEPS, DOWN_UNITS, d0, 3 * l)
                post(3 * l)
                last_split(phase[3 * l] + 2 * GU_STEPS, DOWN_UNITS, 3 * l)
                pre(3 * l + 1)
                mixer(l, 3 * l + 1)
                down_splits(phase[3 * l + 1] + MIX_IN[l], 4, d0 + DOWN_UNITS - 1, 3 * l + 1)
                post(3 * l + 1)
                last_split(phase[3 * l + 1] + MIX_IN[l], 4, 3 * l + 1)
                pre(3 * l + 2)
                gate_up(2 * l + 1, phase[3 * l + 2], NW_PRE[3 * l + 2])
                down_splits(phase[3 * l + 2] + 2 * GU_STEPS, DOWN_UNITS, d0 + DOWN_UNITS - 1 + 3, 3 * l + 2)
                post(3 * l + 2)
                last_split(phase[3 * l + 2] + 2 * GU_STEPS, DOWN_UNITS, 3 * l + 2)
                if l + 1 < LAYERS:
                    pre(3 * l + 3)

        @block.vector
        def _(dve):
            TT, STT, TS = nc.vector.tensor_tensor, nc.vector.scalar_tensor_tensor, nc.vector.tensor_scalar
            gains = [0]

            def split_lo(n, reg=None):
                w = unit_width(n)
                dve.wait_ge(hi_ready, n + 1 if reg is None else reg + 1)
                TT(wsp[n % 2][:, 1, 0:w], raw[n % 2][:, 0:w], wsp[n % 2][:, 0, 0:w].bitcast(F32), ALU.subtract).then_inc(lo_ready, 1)

            def ada_low(slot, count):
                dve.wait_ge(ada_hi_ready, count)
                TT(ada_lo[:, slot, :, :], ada_raw[:, slot, :, :], ada_hi[:].bitcast(F32), ALU.subtract).then_inc(ada_lo_ready, 1)

            def ada_out(block, bank):
                dve.wait_ge(ada_flip, block + 1)
                m = bass.ds((ADA_PRO + block) * ADA_CH, ADA_CH)
                bias = cols[:, m].rearrange("p (a b) -> p a b", b=1).broadcast_to([P, ADA_CH, 2])
                got = ps[bank][:, 0:2 * ADA_CH].rearrange("p (a b) -> p a b", b=2)
                TT(mod[:, m, :], got, bias, ALU.add).then_inc(mod_ready, 1)

            def norm_cols(l, i):
                g = cols[:, C_NORM + l * 48 + i * 8:C_NORM + l * 48 + i * 8 + 8]
                return g.rearrange("p (a b) -> p a b", b=1).broadcast_to([P, KD, 2])

            def invert(count, w):
                dve.wait_ge(root_ready, count)
                nc.vector.reciprocal(rinv[:, 0:w // P], rcol[:, 0:w // P]).then_inc(inv_ready, 1)
                dve.wait_ge(inv_ready, count)
                for t in range(w // P):
                    last = TS(T[2][:, t * P:(t + 1) * P], ident, rinv[:, t:t + 1], None, ALU.mult)
                last.then_inc(diag_ready, 1)

            def gain(ins):
                gains[0] += 1
                ins.then_inc(gain_ready, 1)

            def post(b, inv):
                w = NW_POST[b]
                l, slot = b // 3, b % 3
                m0_ = l * 72 + slot * 24 + 16
                dve.wait_ge(mod_ready, ada_blocks(m0_ + 8))
                gain(STT(gcol[:], mod[:, m0_:m0_ + 8, :], 1.0 if slot == 1 else 0.5, norm_cols(l, 2 * slot + 1), ALU.mult, ALU.mult))
                for ch in range(KD):
                    dve.wait_ge(y_done, KD * b + ch + 1)
                    nc.vector.tensor_copy(Ysb[:, ch, 0:w], ps[bank_of(ch)][:, 0:w]).then_inc(y_out, 1)
                dve.wait_ge(gain_ready, gains[0])
                invert(inv, w)
                dve.wait_ge(spread, inv)
                R = ps[SS1]
                for ch in range(KD):
                    for s in range(w // LAT):
                        c_ = slice(s * LAT, (s + 1) * LAT)
                        last = STT(Ysb[:, ch, c_], Ysb[:, ch, c_], gcol[:, ch, s:s + 1], R[:, c_], ALU.mult, ALU.mult)
                    last.then_inc(upd_ready, 1)
                dve.wait_ge(upd_ready, KD * (b + 1))
                for ch in range(POOL_CH, KD):
                    TT(X[:, ch, 0:w], X[:, ch, 0:w], Ysb[:, ch, 0:w], ALU.add).then_inc(xd_ready, 1)

            def pre(r, inv):
                w = NW_PRE[r]
                l, slot = r // 3, r % 3
                m0_ = l * 72 + slot * 24
                dve.wait_ge(mod_ready, ada_blocks(m0_ + 16))
                gain(STT(scol[:], mod[:, m0_ + 8:m0_ + 16, :], 1.0, norm_cols(l, 2 * slot), ALU.add, ALU.mult))
                dve.wait_ge(gain_ready, gains[0])
                if r:
                    invert(inv, w)
                dve.wait_ge(spread, inv)
                R = ps[SS2]

                def high(ch):
                    dve.wait_ge(hv_ready, KD * r + ch + 1)
                    nc.vector.tensor_copy(H[:, ch, 0, 0:w], h_whole[:, ch, 1, 0:w]).then_inc(hh_ready, 1)

                for ch in range(KD):
                    TT(h_whole[:, ch, 1, 0:w], X[:, ch, 0:w], R[:, 0:w], ALU.mult).then_inc(ht_ready, 1)
                    if ch >= 2:
                        high(ch - 2)
                high(KD - 2)
                high(KD - 1)
                for ch in range(POOL_CH, KD):
                    dve.wait_ge(hh_ready, KD * r + ch + 1)
                    TT(H[:, ch, 1, 0:w], h_whole[:, ch, 1, 0:w], H[:, ch, 0, 0:w].bitcast(F32), ALU.subtract).then_inc(hd_ready, 1)
                if r:
                    ada_out(ada_norm[r], B_ADA_NORM)

            def gate_up(q, n0, w, l, s):
                def steps(lo_, hi_, with_ada):
                    with dve.Fori(lo_, hi_) as i:
                        if with_ada:
                            ada_low(1, ADA_PCS * i + 2)
                            ada_low(0, ADA_PCS * i + 3)
                        split_lo(n0 + 2, n0 + 2 + 2 * i)
                        if with_ada:
                            ada_low(1, ADA_PCS * i + 4)
                        for j in range(2):
                            dve.wait_ge(up_done, q * NF + 2 * i + j + 1)
                            dve.wait_ge(silu_done, q * NF + 2 * i + j + 3)
                            TT(T[j][:, 0:w], ps[2 + j][:, 0:w], T[j][:, 0:w], ALU.mult).then_inc(prod_done, 1)
                        if with_ada:
                            ada_out(i, 4)
                            ada_low(0, ADA_PCS * i + 5)
                        for j in range(2):
                            dve.wait_ge(ahi_done, q * NF + 2 * i + j + 1)
                            o = A[:, bass.ds(2 * i + j, 1), 1, 0:w].rearrange("p a n -> p (a n)")
                            hi = A[:, bass.ds(2 * i + j, 1), 0, 0:w].rearrange("p a n -> p (a n)")
                            TT(o, T[j][:, 0:w], hi.bitcast(F32), ALU.subtract).then_inc(alo_done, 1)
                        split_lo(n0 + 3, n0 + 3 + 2 * i)

                if q == 0:
                    steps(0, ADA_FFN, True)
                steps(ADA_FFN if q == 0 else 0, GU_STEPS, False)

            def down_splits(n1, units):
                if units == DOWN_UNITS:
                    for u in range(2):
                        split_lo(n1 + u + 2)
                    with dve.Fori(1, 4) as i:
                        for j in range(2):
                            split_lo(n1 + 2 + j, n1 + 2 + j + 2 * i)
                    rest = (8, 9)
                else:
                    rest = range(units - 1)
                for u in rest:
                    if n1 + u + 2 < last_unit:
                        split_lo(n1 + u + 2)

            def last_split(n1, units):
                if n1 + units + 1 < last_unit:
                    split_lo(n1 + units + 1)

            def mixer(l, b):
                toks, items, pe, ac, st = plans[l]
                n0 = phase[b]
                mc = (mc0, mc1)[l]
                qh, kh, pp = (qh0, kh0, probs[0]) if l == 0 else (qh1, None, probs[1])
                kd_ = (kdup0, kdup1)[l]
                tiles = 4 if l == 0 else 2
                dve.wait_ge(mix_in, 16 * (l + 1))
                dve.wait_ge(sink_in, 16)
                for t in toks:
                    k = t[0]
                    if k == "flip":
                        ada_out(t[1], B_ADA)
                    elif k == "proj":
                        o = work_bank(l, t)
                        what, j = t[1:]
                        dve.wait_ge(pe_step, pe.at(*t))
                        if what == "q":
                            if j >= 4:
                                dve.wait_ge(pe_step, pe.at("score", (j // 2 - 1) * 8 - 1))
                            last = TS(qh[j % 4][0:QK, :], o[0:QK, :], MLA_SCALE, None, ALU.mult)
                        elif what == "k":
                            if j >= 4:
                                dve.wait_ge(pe_step, pe.at("score", (j // 2 - 1) * 8 - 1))
                            last = nc.vector.tensor_copy(kh[j % 4][0:HD, :], o[0:HD, :])
                        elif (l, what) == (0, "cq"):
                            last = nc.vector.tensor_copy(qh[j][:], o[:])
                        elif what == "ckv":
                            last = nc.vector.tensor_copy(qh[2][:], o[:])
                        elif what == "kr":
                            nc.vector.memset(T[3][0:HD, 0:LAT], 0.0)
                            last = nc.vector.tensor_copy(T[3][HD:QK, :], o[0:32, :])
                        elif what == "va":
                            last = nc.vector.tensor_copy(va[:, j, :], o[:])
                        elif what in ("bk", "ck"):
                            if what == "bk":
                                dve.wait_ge(pe_step, pe.at("score", 8 * 3 - 1))
                            last = nc.vector.tensor_copy(kbuf[what][:], o[:])
                        elif what in ("bv", "cv"):
                            last = nc.vector.tensor_copy(vbuf[what][:, 0:NT], o[:])
                        elif what == "bq":
                            if j == 4 or j == 5:
                                dve.wait_ge(pe_step, pe.at("score", 8 * 4 - 1) if j == 5 else pe.at("score", 8 * 3 - 1))
                            else:
                                dve.wait_ge(pe_step, pe.at("score", (j - 1) * 8 - 1))
                            dve.wait_ge(act_step, ac.at("square", "bq", j, 0))
                            last = TS(qh[j % 2][:], o[:], cols[:, C_GQ:C_GQ + 1], None, ALU.mult)
                        elif what == "dv":
                            u, half = j // 2, j % 2
                            last = nc.vector.tensor_copy(dv[:, 2 * half:2 * half + 2, u * 256:(u + 1) * 256],
                                                         o[:].rearrange("p (a n) -> p a n", a=2))
                        elif what == "dk":
                            last = nc.vector.tensor_copy(dk[:, j, :], o[:])
                        else:
                            if j >= 2:
                                dve.wait_ge(pe_step, pe.at("score", (j - 1) * 4 - 1))
                            last = TS(qh[j % 2][:], o[:, 0:LAT], HD_SCALE, None, ALU.mult)
                        st.did(dve_step, last, *t)
                    elif k == "turnv":
                        dve.wait_ge(pe_step, pe.at(*t))
                        o = (vb if l == 0 else cv)[:, :, :].rearrange("p a n -> p (a n)")
                        st.did(dve_step, nc.vector.tensor_copy(o, work_bank(l, t)[:]), *t)
                    elif k == "norm" and t[1] == "bq":
                        p = t[2]
                        dve.wait_ge(pe_step, pe.at("sum", "bq", p))
                        if p >= 6:
                            dve.wait_ge(rq_ready, p - 5)
                        st.did(dve_step, TS(ssq[:, p % 2, :], work_bank(l, ("sum", "bq", p))[:, 0:8], HD * EPS, None, ALU.add),
                               "squares", "bq", p)
                    elif k in ("rank", "norm"):
                        what, j = t[1:]
                        n = 2 if what == "cq" else 1
                        dve.wait_ge(act_step, ac.at("root", what, j))
                        st.did(dve_step, nc.vector.reciprocal(Rm[:], Rm[:]), "inv", what, j)
                        dve.wait_ge(dve_step, st.at("inv", what, j))
                        if k == "norm":
                            src = kbuf[what]
                            st.did(dve_step, STT(src[:], src[:], cols[:, C_GK:C_GK + 1], Rm[:], ALU.mult, ALU.mult), "normed", what, j)
                        else:
                            src = [qh[0], qh[1]] if what == "cq" else [qh[2]]
                            g0 = C_QN if what == "cq" else C_KVN
                            for i in range(n):
                                st.did(dve_step, STT(src[i][:], src[i][:], cols[:, g0 + i:g0 + i + 1], Rm[:], ALU.mult, ALU.mult),
                                       "scaled", what, i)
                            for i in range(n):
                                hi, lo_ = (cqn[:, i, 0, :], cqn[:, i, 1, :]) if what == "cq" else (ckvn[:, 0, :], ckvn[:, 1, :])
                                dve.wait_ge(act_step, ac.at("hi", what, i))
                                st.did(dve_step, TT(lo_, src[i][:], hi.bitcast(F32), ALU.subtract), "lo", what, i)
                    elif k == "rope":
                        what, j = t[1:]
                        if what in ("q", "kr"):
                            g, cc, ss = slice(HD, QK), M_C96, M_S96
                            tgt = qh[j % 4] if what == "q" else T[3]
                        else:
                            g, cc, ss = slice(0, P), M_C64, M_S64
                            tgt = kbuf.get(what, qh[j % 2])
                        dve.wait_ge(pe_step, pe.at(*t))
                        st.did(dve_step, TT(T[0][g, 0:LAT], work_bank(l, t)[g, 0:LAT], mc[g, ss:ss + LAT], ALU.mult), "sin", what, j)
                        st.did(dve_step, TT(T[1][g, 0:LAT], tgt[g, 0:LAT], mc[g, cc:cc + LAT], ALU.mult), "cos", what, j)
                        dve.wait_ge(dve_step, st.at("cos", what, j))
                        st.did(dve_step, TT(tgt[g, 0:LAT], T[0][g, 0:LAT], T[1][g, 0:LAT], ALU.add), *t)
                    elif k == "dup":
                        dve.wait_ge(dve_step, st.at("rope", *t[1:]))
                        if t[1] == "kr":
                            for i in range(4):
                                last = nc.vector.tensor_copy(kh[i][HD:QK, :], T[3][HD:QK, :])
                        else:
                            for g in range(2):
                                for half in range(2):
                                    last = nc.vector.tensor_copy(kd_[g][half * HD:(half + 1) * HD, :], kbuf[t[1]][g * HD:(g + 1) * HD, :])
                        st.did(dve_step, last, *t)
                    elif k == "score":
                        i = t[1]
                        p, e, tt = items[i]
                        k0_ = 0 if tt < 2 else LAT
                        S = ps[B_S[i % DEEP]]
                        dve.wait_ge(pe_step, pe.at(*t))
                        if l == 1:
                            if i == 16:
                                dve.wait_ge(toe_ready, 8)
                            bias = mc[:, M_SWA + tt * LAT:M_SWA + (tt + 1) * LAT] if p < 4 else \
                                toe[:, 2 * (p - 4) + e, 2 - 2 * tt + 0:6 - 2 * tt, :].rearrange("p a n -> p (a n)")
                            st.did(dve_step, TT(S[:, 0:LAT], S[:, 0:LAT], bias, ALU.add), "bias", i)
                            dve.wait_ge(dve_step, st.at("bias", i))
                        if i >= DEEP:
                            dve.wait_ge(act_step, ac.at("sinkexp" if l == 1 and i - DEEP < 16 else "exp", i - DEEP))
                        sink = l == 1 and i < 16
                        if l == 0 and i >= 32:
                            m = smax[:, i % DEEP:i % DEEP + 1]
                            st.did(dve_step, nc.vector.tensor_reduce(m, S[:, k0_:NT], AX_X, ALU.max), "max", i)
                            dve.wait_ge(dve_step, st.at("max", i))
                            if i % 8 == 0:
                                dve.wait_ge(rq_ready, p - 3)
                            st.did(dve_step, TS(nmax[:, i % DEEP:i % DEEP + 1], m, rq[:, p % 2, 2 * tt + e:2 * tt + e + 1], -1.0, ALU.mult, ALU.mult),
                                   "scaledmax", i)
                        elif sink:
                            m = smax[:, i % DEEP:i % DEEP + 1]
                            st.did(dve_step, nc.vector.tensor_reduce(m, S[:, k0_:NT], AX_X, ALU.max), "max", i)
                            dve.wait_ge(dve_step, st.at("max", i))
                            st.did(dve_step, TS(nmax[:, i % DEEP:i % DEEP + 1], m, sinkc[:, 2 * p + e:2 * p + e + 1], -1.0, ALU.max, ALU.mult),
                                   "sinkmax", i)
                        else:
                            st.did(dve_step, nc.vector.tensor_reduce(nmax[:, i % DEEP:i % DEEP + 1], S[:, k0_:NT], AX_X, ALU.max, negate=True),
                                   "max", i)
                    elif k == "prob":
                        i = t[1]
                        k0_ = 0 if items[i][2] < 2 else LAT
                        tot = psum_[:, i % DEEP:i % DEEP + 1]
                        if l == 1 and i < 16:
                            dve.wait_ge(act_step, ac.at("sinkexp", i))
                            st.did(dve_step, TT(smax[:, i % DEEP:i % DEEP + 1], tot, sexp[:, i % DEEP:i % DEEP + 1], ALU.add), "total", i)
                            dve.wait_ge(dve_step, st.at("total", i))
                            tot = smax[:, i % DEEP:i % DEEP + 1]
                        else:
                            dve.wait_ge(act_step, ac.at("exp", i))
                        st.did(dve_step, nc.vector.reciprocal(pinv[:, i % DEEP:i % DEEP + 1], tot), "inv", i)
                        dve.wait_ge(dve_step, st.at("inv", i))
                        st.did(dve_step, TS(pp[i % DEEP][:, k0_:NT], pp[i % DEEP][:, k0_:NT], pinv[:, i % DEEP:i % DEEP + 1], None, ALU.mult), "prob", i)
                    elif k == "out":
                        p = t[1]
                        w = NW_POST[b]
                        dve.wait_ge(act_step, ac.at("out", p))
                        st.did(dve_step, TT(A[:, p, 1, 0:w], ps[B_O][:, 0:w], A[:, p, 0, 0:w].bitcast(F32), ALU.subtract), "out", p)

            nc.vector.memset(sT[:, :, 2:4], 0.0)
            nc.vector.memset(epsc[:], EPS).then_inc(zero_ready, 1)
            dve.sem_inc(prod_done, 2)
            dve.sem_inc(alo_done, 2)
            for i, (c0, n) in enumerate(((0, P), (P, P), (2 * P, 5))):
                dve.wait_ge(rows_t, i + 1)
                nc.vector.tensor_copy(cols[:, c0:c0 + n], ps[i][:, 0:n]).then_inc(cols_ready, 1)
            dve.wait_ge(cols_ready, 3)
            dve.wait_ge(consts_in, 16)
            TT(fold[:], ident[0:4, 0:2], ident[0:4, 2:4], ALU.add)
            dve.wait_ge(s_split, 1)
            TT(sS[:, :, 2:4], sT[:, :, 0:2], sS[:, :, 0:2].bitcast(F32), ALU.subtract).then_inc(s_split, 1)
            for i, ch in enumerate((3, 4, 5, 6, 7, 0, 1, 2)):
                dve.wait_ge(xt_done, i + 1)
                nc.vector.tensor_copy(X[:, ch, :], ps[ch][:]).then_inc(x_loaded, 1)
            invert(1, NT)
            for i in (2, 3):
                c_ = slice(i * ADA_W, (i + 1) * ADA_W)
                dve.wait_ge(pro_hi_ready, i - 1)
                TT(pro_lo[:, :, c_], ada_pro[:, :, c_], pro_his[i - 2][:, :, :].bitcast(F32), ALU.subtract).then_inc(pro_lo_ready, 1)
            ada_low(0, 1)
            split_lo(0)
            dve.wait_ge(pro_flip, 1)
            n = ADA_PRO * ADA_CH
            bias = cols[:, 0:n].rearrange("p (a b) -> p a b", b=1).broadcast_to([P, n, 2])
            got = ps[PRO_BANKS[0]][:, 0:2 * n].rearrange("p (a b) -> p a b", b=2)
            TT(mod[:, 0:n, :], got, bias, ALU.add).then_inc(mod_ready, 1)
            dve.wait_ge(mod_ready, 1)
            pre(0, 1)
            split_lo(1)
            for l in range(LAYERS):
                for s in range(2):
                    b = 3 * l + 2 * s
                    gate_up(2 * l + s, phase[b], NW_PRE[b], l, s)
                    n1 = phase[b] + 2 * GU_STEPS
                    down_splits(n1, DOWN_UNITS)
                    post(b, 2 * b + 2)
                    last_split(n1, DOWN_UNITS)
                    if b < 5:
                        pre(b + 1, 2 * b + 3)
                    if s == 0:
                        mixer(l, b + 1)
                        n1 = phase[b + 1] + MIX_IN[l]
                        down_splits(n1, 4)
                        post(b + 1, 2 * b + 4)
                        last_split(n1, 4)
                        pre(b + 2, 2 * b + 5)
            for i in range(4):
                dve.wait_ge(ot_done, i + 1)
                t, half = i // 2, i % 2
                nc.vector.tensor_copy(outs[:, t, half * 512:(half + 1) * 512], ps[i][:]).then_inc(o_ready, 1)


_INS = ['x', 'c', 'ctx', 'c_ctx', 'ada_w', 'ada_b', 'norm_g', 'ffn_w_gate', 'ffn_w_up', 'ffn_w_down',
        'ab_w_in', 'mla_q_norm', 'mla_w_uq', 'mla_kv_norm', 'mla_w_ukv', 'gqa_q_norm', 'gqa_k_norm',
        'ab_w_out', 'cd_w_in', 'swa_sink', 'na_rpb', 'cd_w_out']


def kernel(**inputs):
    import numpy as _np
    import concourse.bacc as _bacc
    from concourse import mybir as _mybir
    from concourse.bass_utils import run_bass_kernel_spmd as _run

    nc = _bacc.Bacc("TRN2", target_bir_lowering=False, num_devices=1)
    arrays, args = {}, []
    for name in _INS:
        a = _np.ascontiguousarray(inputs[name])
        arrays[f"in_{name}"] = a
        args.append(nc.dram_tensor(f"in_{name}", a.shape, _mybir.dt.from_np(a.dtype), kind="ExternalInput").ap())
    k = constants()
    arrays["in_consts"] = k
    args.append(nc.dram_tensor("in_consts", k.shape, _mybir.dt.float32, kind="ExternalInput").ap())
    args.append(nc.dram_tensor("out_0", (1, LAT, D), _mybir.dt.float32, kind="ExternalOutput").ap())
    dit_kernel(nc, *args)
    r = _run(nc, [arrays], core_ids=[0])
    return r.results[0]["out_0"]
```
